# Optimizing a Trainium2 kernel written in Bass

```python
import math
import jax, jax.numpy as jnp
from jax import lax
import numpy as np

D_MODEL = 1024
BATCH = 1
SEQ = 512
DEPTH = 1
DEC_BATCH = 8
DEC_SEQ = 8
PAST_LEN = 4096
PAGE_SIZE = 128

EPS = 1e-6
D_FF = ((8 * D_MODEL // 3 + 127) // 128) * 128
GLA_WIDTH = D_MODEL // 2
GLA_HEADS = 4
GLA_DV = GLA_WIDTH // GLA_HEADS
GLA_DK = GLA_DV // 2
GLA_QK_WIDTH = GLA_HEADS * GLA_DK
GLA_GATE_RANK = 16
GLA_TAU = 16.0
GLA_CHUNK = 16
S5_WIDTH = D_MODEL - GLA_WIDTH
S5_P = 16
S5_GROUPS = S5_WIDTH // S5_P
S5_N = 64
S5_DT_MIN = 0.001
S5_DT_MAX = 0.1
MIX_WIDTH = GLA_WIDTH + S5_WIDTH
CROSS_HEADS = 4
CROSS_DH = D_MODEL // CROSS_HEADS
MEM_LEN = 256
IN_SIZES = (GLA_QK_WIDTH, GLA_QK_WIDTH, GLA_WIDTH, GLA_GATE_RANK, GLA_WIDTH, S5_WIDTH)
IN_WIDTH = sum(IN_SIZES)
SPLIT_POINTS = tuple(int(s) for s in np.cumsum(IN_SIZES)[:-1])

kernel_name = "hymba_gla_s5_macaron_decode_step"

def rms_norm(x, g):
    xf = x.astype(jnp.float32)
    y = xf * lax.rsqrt(jnp.mean(xf * xf, axis=-1, keepdims=True) + EPS)
    return (y * g.astype(jnp.float32)).astype(x.dtype)

def swiglu(x, w_gu, w_down):
    g, u = jnp.split(x @ w_gu, 2, axis=-1)
    return (jax.nn.silu(g) * u) @ w_down

def gla_recurrence(q, k, v, log_a, s0):
    bsz, t, h, _ = q.shape
    dv = v.shape[-1]
    n_chunks = -(-t // GLA_CHUNK)
    pad = n_chunks * GLA_CHUNK - t

    def to_chunks(a):
        a = jnp.pad(a, ((0, 0), (0, pad), (0, 0), (0, 0)))
        return a.reshape(bsz, n_chunks, GLA_CHUNK, h, a.shape[-1]).transpose(1, 0, 3, 2, 4)

    qc, kc, vc, lc = to_chunks(q), to_chunks(k), to_chunks(v), to_chunks(log_a)
    bc = jnp.cumsum(lc, axis=3)
    causal = jnp.tril(jnp.ones((GLA_CHUNK, GLA_CHUNK), dtype=bool))[:, :, None]

    def step(s, inp):
        qi, ki, vi, bi = inp
        o_inter = jnp.einsum('bhtd,bhde->bhte', qi * jnp.exp(bi), s)
        rel = bi[:, :, :, None, :] - bi[:, :, None, :, :]
        decay = jnp.exp(jnp.where(causal, rel, -jnp.inf))
        scores = jnp.einsum('bhtd,bhsd,bhtsd->bhts', qi, ki, decay)
        o_intra = jnp.einsum('bhts,bhse->bhte', scores, vi)
        b_last = bi[:, :, -1:, :]
        s_new = jnp.exp(b_last[:, :, 0, :])[..., None] * s + jnp.einsum(
            'bhsd,bhse->bhde', ki * jnp.exp(b_last - bi), vi)
        return s_new, o_inter + o_intra

    s_final, o = lax.scan(step, s0, (qc, kc, vc, bc))
    o = o.transpose(1, 0, 3, 2, 4).reshape(bsz, n_chunks * GLA_CHUNK, h, dv)[:, :t]
    return o, s_final

def s5_discretise(lambda_re, lambda_im, log_dt, b_re, b_im):
    lr = lambda_re.astype(jnp.float32)
    li = lambda_im.astype(jnp.float32)
    dt = jnp.exp(log_dt.astype(jnp.float32))[:, None]
    mag = jnp.exp(dt * lr)
    ab_re = mag * jnp.cos(dt * li)
    ab_im = mag * jnp.sin(dt * li)
    den = lr * lr + li * li
    coef_re = ((ab_re - 1.0) * lr + ab_im * li) / den
    coef_im = (ab_im * lr - (ab_re - 1.0) * li) / den
    br = b_re.astype(jnp.float32)
    bi = b_im.astype(jnp.float32)
    bb_re = coef_re[..., None] * br - coef_im[..., None] * bi
    bb_im = coef_re[..., None] * bi + coef_im[..., None] * br
    return ab_re, ab_im, bb_re, bb_im

def complex_affine_combine(e1, e2):
    a1r, a1i, b1r, b1i = e1
    a2r, a2i, b2r, b2i = e2
    return (a2r * a1r - a2i * a1i,
            a2r * a1i + a2i * a1r,
            a2r * b1r - a2i * b1i + b2r,
            a2r * b1i + a2i * b1r + b2i)

def s5_mixer(u, x0_re, x0_im, lambda_re, lambda_im, log_dt, b_re, b_im, c_re, c_im, d_skip, w_glu, b_glu):
    ab_re, ab_im, bb_re, bb_im = s5_discretise(lambda_re, lambda_im, log_dt, b_re, b_im)
    bu_re = jnp.einsum('btgp,gnp->btgn', u, bb_re)
    bu_im = jnp.einsum('btgp,gnp->btgn', u, bb_im)
    first_re = bu_re[:, :1] + (ab_re * x0_re - ab_im * x0_im)[:, None]
    first_im = bu_im[:, :1] + (ab_re * x0_im + ab_im * x0_re)[:, None]
    bu_re = jnp.concatenate([first_re, bu_re[:, 1:]], axis=1)
    bu_im = jnp.concatenate([first_im, bu_im[:, 1:]], axis=1)
    a_re = jnp.broadcast_to(ab_re, bu_re.shape)
    a_im = jnp.broadcast_to(ab_im, bu_im.shape)
    _, _, xr, xi = lax.associative_scan(complex_affine_combine, (a_re, a_im, bu_re, bu_im), axis=1)
    y = (jnp.einsum('btgn,gpn->btgp', xr, c_re.astype(jnp.float32))
         - jnp.einsum('btgn,gpn->btgp', xi, c_im.astype(jnp.float32))
         + d_skip.astype(jnp.float32) * u)
    z = jax.nn.gelu(y)
    out = z * jax.nn.sigmoid(jnp.einsum('btgp,gpq->btgq', z, w_glu.astype(jnp.float32))
                             + b_glu.astype(jnp.float32))
    return out, xr[:, -1], xi[:, -1]

def memory_kv(mem, g_mem, w_ckv):
    bsz = mem.shape[0]
    k, v = jnp.split(rms_norm(mem, g_mem) @ w_ckv, 2, axis=-1)
    return (k.reshape(bsz, MEM_LEN, CROSS_HEADS, CROSS_DH),
            v.reshape(bsz, MEM_LEN, CROSS_HEADS, CROSS_DH))

def cross_attend(xn, mem_k, mem_v, w_cq, w_co):
    bsz, t, _ = xn.shape
    q = (xn @ w_cq).reshape(bsz, t, CROSS_HEADS, CROSS_DH)
    s = jnp.einsum('bthd,bmhd->bhtm', q, mem_k).astype(jnp.float32) * (CROSS_DH ** -0.5)
    p = jax.nn.softmax(s, axis=-1).astype(mem_v.dtype)
    o = jnp.einsum('bhtm,bmhd->bthd', p, mem_v).reshape(bsz, t, D_MODEL)
    return o @ w_co

def trunk_layer(x, s_gla0, s5_re0, s5_im0, mem_k, mem_v, w):
    bsz, t, _ = x.shape
    f32 = jnp.float32
    h = x + 0.5 * swiglu(rms_norm(x, w['g_ffn1']), w['w_ffn1_gu'], w['w_ffn1_down'])
    u = rms_norm(h, w['g_mix'])
    q, k, v, zg, r, us5 = jnp.split(u @ w['w_in'], SPLIT_POINTS, axis=-1)
    q = q.reshape(bsz, t, GLA_HEADS, GLA_DK).astype(f32) * (GLA_DK ** -0.5)
    k = k.reshape(bsz, t, GLA_HEADS, GLA_DK).astype(f32)
    v = v.reshape(bsz, t, GLA_HEADS, GLA_DV).astype(f32)
    log_a = jax.nn.log_sigmoid(zg.astype(f32) @ w['w_gla_gate'].astype(f32)
                               + w['b_gla_gate'].astype(f32)) / GLA_TAU
    log_a = log_a.reshape(bsz, t, GLA_HEADS, GLA_DK)
    o, s_gla = gla_recurrence(q, k, v, log_a, s_gla0.astype(f32))
    o = rms_norm(o, w['g_gla_out']) * jax.nn.silu(r.reshape(bsz, t, GLA_HEADS, GLA_DV).astype(f32))
    o_s5, s5_re, s5_im = s5_mixer(
        us5.reshape(bsz, t, S5_GROUPS, S5_P).astype(f32), s5_re0.astype(f32), s5_im0.astype(f32),
        w['s5_lambda_re'], w['s5_lambda_im'], w['s5_log_dt'], w['s5_b_re'], w['s5_b_im'],
        w['s5_c_re'], w['s5_c_im'], w['s5_d'], w['s5_w_glu'], w['s5_b_glu'])
    mix = jnp.concatenate([o.reshape(bsz, t, GLA_WIDTH), o_s5.reshape(bsz, t, S5_WIDTH)], axis=-1)
    h = h + mix.astype(x.dtype) @ w['w_out']
    h = h + cross_attend(rms_norm(h, w['g_cross']), mem_k, mem_v, w['w_cq'], w['w_co'])
    h = h + 0.5 * swiglu(rms_norm(h, w['g_ffn2']), w['w_ffn2_gu'], w['w_ffn2_down'])
    return h, s_gla, s5_re, s5_im

def setup_inputs(seed: int = 0) -> dict:
    key = jax.random.key(seed)
    ks = iter(jax.random.split(key, 48))
    f32 = jnp.float32

    def nrm(shape, scale):
        return jax.random.normal(next(ks), shape, f32) * scale

    def gain(shape):
        return jnp.ones(shape, f32) + nrm(shape, 0.02)

    L = DEPTH
    inp = {}
    inp['x_prompt'] = nrm((BATCH, SEQ, D_MODEL), 1.0)
    inp['x_sample'] = nrm((DEC_BATCH, DEC_SEQ, D_MODEL), 1.0)
    inp['state_gla'] = nrm((L, DEC_BATCH, GLA_HEADS, GLA_DK, GLA_DV), 1.0)
    inp['state_s5_re'] = nrm((L, DEC_BATCH, S5_GROUPS, S5_N), 0.1)
    inp['state_s5_im'] = nrm((L, DEC_BATCH, S5_GROUPS, S5_N), 0.1)
    inp['cache_mem_k'] = nrm((L, DEC_BATCH, MEM_LEN, CROSS_HEADS, CROSS_DH), 1.0)
    inp['cache_mem_v'] = nrm((L, DEC_BATCH, MEM_LEN, CROSS_HEADS, CROSS_DH), 1.0)
    inp['mem_prompt'] = nrm((BATCH, MEM_LEN, D_MODEL), 1.0)
    inp['g_ffn1'] = gain((L, D_MODEL))
    inp['w_ffn1_gu'] = nrm((L, D_MODEL, 2 * D_FF), D_MODEL ** -0.5)
    inp['w_ffn1_down'] = nrm((L, D_FF, D_MODEL), D_FF ** -0.5)
    inp['g_mix'] = gain((L, D_MODEL))
    inp['w_in'] = nrm((L, D_MODEL, IN_WIDTH), D_MODEL ** -0.5)
    inp['w_gla_gate'] = nrm((L, GLA_GATE_RANK, GLA_QK_WIDTH), GLA_GATE_RANK ** -0.5)
    inp['b_gla_gate'] = nrm((L, GLA_QK_WIDTH), 0.1)
    inp['g_gla_out'] = gain((L, GLA_DV))
    inp['s5_lambda_re'] = -0.5 + nrm((L, S5_GROUPS, S5_N), 0.01)
    inp['s5_lambda_im'] = (math.pi * jnp.broadcast_to(jnp.arange(S5_N, dtype=f32), (L, S5_GROUPS, S5_N))
                           + nrm((L, S5_GROUPS, S5_N), 0.01))
    inp['s5_log_dt'] = jax.random.uniform(next(ks), (L, S5_GROUPS), f32,
                                          math.log(S5_DT_MIN), math.log(S5_DT_MAX))
    inp['s5_b_re'] = nrm((L, S5_GROUPS, S5_N, S5_P), (2.0 * S5_P) ** -0.5)
    inp['s5_b_im'] = nrm((L, S5_GROUPS, S5_N, S5_P), (2.0 * S5_P) ** -0.5)
    inp['s5_c_re'] = nrm((L, S5_GROUPS, S5_P, S5_N), (2.0 * S5_N) ** -0.5)
    inp['s5_c_im'] = nrm((L, S5_GROUPS, S5_P, S5_N), (2.0 * S5_N) ** -0.5)
    inp['s5_d'] = nrm((L, S5_GROUPS, S5_P), 1.0)
    inp['s5_w_glu'] = nrm((L, S5_GROUPS, S5_P, S5_P), S5_P ** -0.5)
    inp['s5_b_glu'] = nrm((L, S5_GROUPS, S5_P), 0.1)
    inp['w_out'] = nrm((L, MIX_WIDTH, D_MODEL), MIX_WIDTH ** -0.5)
    inp['g_cross'] = gain((L, D_MODEL))
    inp['g_mem'] = gain((L, D_MODEL))
    inp['w_cq'] = nrm((L, D_MODEL, D_MODEL), D_MODEL ** -0.5)
    inp['w_ckv'] = nrm((L, D_MODEL, 2 * D_MODEL), D_MODEL ** -0.5)
    inp['w_co'] = nrm((L, D_MODEL, D_MODEL), D_MODEL ** -0.5)
    inp['g_ffn2'] = gain((L, D_MODEL))
    inp['w_ffn2_gu'] = nrm((L, D_MODEL, 2 * D_FF), D_MODEL ** -0.5)
    inp['w_ffn2_down'] = nrm((L, D_FF, D_MODEL), D_FF ** -0.5)
    inp['g_final'] = gain((D_MODEL,))
    return inp

def reference(x_prompt, x_sample, state_gla, state_s5_re, state_s5_im, cache_mem_k, cache_mem_v,
              mem_prompt, g_ffn1, w_ffn1_gu, w_ffn1_down, g_mix, w_in, w_gla_gate, b_gla_gate,
              g_gla_out, s5_lambda_re, s5_lambda_im, s5_log_dt, s5_b_re, s5_b_im, s5_c_re, s5_c_im,
              s5_d, s5_w_glu, s5_b_glu, w_out, g_cross, g_mem, w_cq, w_ckv, w_co, g_ffn2,
              w_ffn2_gu, w_ffn2_down, g_final):
    bp = x_prompt.shape[0]
    f32 = jnp.float32
    hp, hs = x_prompt, x_sample
    gla_p, re_p, im_p, mk_p, mv_p = [], [], [], [], []
    gla_s, re_s, im_s = [], [], []
    for l in range(DEPTH):
        w = {
            'g_ffn1': g_ffn1[l], 'w_ffn1_gu': w_ffn1_gu[l], 'w_ffn1_down': w_ffn1_down[l],
            'g_mix': g_mix[l], 'w_in': w_in[l], 'w_gla_gate': w_gla_gate[l], 'b_gla_gate': b_gla_gate[l],
            'g_gla_out': g_gla_out[l], 's5_lambda_re': s5_lambda_re[l], 's5_lambda_im': s5_lambda_im[l],
            's5_log_dt': s5_log_dt[l], 's5_b_re': s5_b_re[l], 's5_b_im': s5_b_im[l],
            's5_c_re': s5_c_re[l], 's5_c_im': s5_c_im[l], 's5_d': s5_d[l], 's5_w_glu': s5_w_glu[l],
            's5_b_glu': s5_b_glu[l], 'w_out': w_out[l], 'g_cross': g_cross[l], 'w_cq': w_cq[l],
            'w_co': w_co[l], 'g_ffn2': g_ffn2[l], 'w_ffn2_gu': w_ffn2_gu[l], 'w_ffn2_down': w_ffn2_down[l],
        }
        mk, mv = memory_kv(mem_prompt, g_mem[l], w_ckv[l])
        hp, sg, sr, si = trunk_layer(
            hp,
            jnp.zeros((bp, GLA_HEADS, GLA_DK, GLA_DV), f32),
            jnp.zeros((bp, S5_GROUPS, S5_N), f32),
            jnp.zeros((bp, S5_GROUPS, S5_N), f32),
            mk, mv, w)
        gla_p.append(sg); re_p.append(sr); im_p.append(si); mk_p.append(mk); mv_p.append(mv)
        hs, sg, sr, si = trunk_layer(hs, state_gla[l], state_s5_re[l], state_s5_im[l],
                                     cache_mem_k[l], cache_mem_v[l], w)
        gla_s.append(sg); re_s.append(sr); im_s.append(si)
    y_prompt = rms_norm(hp, g_final)
    y_sample = rms_norm(hs, g_final)
    return (y_prompt, y_sample,
            jnp.stack(gla_p), jnp.stack(re_p), jnp.stack(im_p), jnp.stack(mk_p), jnp.stack(mv_p),
            jnp.stack(gla_s), jnp.stack(re_s), jnp.stack(im_s))


_drawn_inputs = setup_inputs


def setup_inputs(seed=0):
    import zlib

    import numpy as np

    out = dict(_drawn_inputs(seed))
    spreads = {}
    factors = {'g_ffn1': 5.317,
     'g_gla_out': 36.258,
     's5_lambda_re': 63.246,
     's5_c_re': 28.823,
     's5_c_im': 27.763,
     's5_b_glu': 89.583,
     'g_cross': 31.514,
     'g_mem': 7.47,
     'g_ffn2': 7.599,
     'g_final': 25.48,
     's5_w_glu': 3.209}
    for name, (base, spread) in spreads.items():
        noise = np.random.default_rng([zlib.crc32(name.encode()), seed]).standard_normal(out[name].shape)
        drawn = base * np.exp(spread * noise) if base else spread * noise
        out[name] = __import__('jax').numpy.asarray(drawn.astype(out[name].dtype))
    for name, factor in factors.items():
        out[name] = (out[name] * factor).astype(out[name].dtype)
    return out
```

```python
import math
from contextlib import ExitStack

import concourse.bass as bass
from concourse import mybir

F32 = mybir.dt.float32
F32R = mybir.dt.float32r
I32 = mybir.dt.int32
ALU = mybir.AluOpType
ACT = mybir.ActivationFunctionType
AX = mybir.AxisListType.X

P = 128
D = 1024
KD = D // P
TP, NB, BT = 512, 8, 8
TS = NB * BT
T = TP + TS
TH = T // 2
NT = (T + P - 1) // P
F = 2816
FT = F // P
FGROUPS = (8, 8, 6)
EPS = 1e-6
H, DK, DV, RANK = 4, 64, 128, 16
TAU = 16.0
CH = 64
LEVELS = (1, 2, 4, 8, 16, 32)
NCH = TP // CH
G, N5, P5 = 32, 64, 16
L5 = 8
C5P = TP // L5
C5 = T // L5
M = 256
CD = 256
TWO_PI = 6.283185307179586
PI_A, PI_B = 6.28125, 0.0019350051879882812
PI_C = TWO_PI - PI_A - PI_B
LN2_HI, LN2_LO = 0.693359375, -2.12194440054690581e-4
ROUND = 12582912.0

MW = 10752
C_ID, C_SCAN, C_MASK, C_CHUNK, C_BATCH = 0, P, P + T, P + T + 7 * CH, P + T + 7 * CH + C5P
C_END = C_BATCH + NB
G_FFN1, G_MIX, G_CROSS, G_FFN2, G_FINAL, G_MEM = range(6)


def hymba_kernel(nc, A, O, consts):
    with ExitStack() as ctx:
        def sb(name, shape, dt=F32):
            return ctx.enter_context(nc.sbuf_tensor(name, shape, dt))

        def alias(name, floats):
            with nc.sbuf_tensor(name, [P, floats], F32) as t:
                return t

        sems = {}

        def S(name):
            if name not in sems:
                sems[name] = ctx.enter_context(nc.semaphore(name))
            return sems[name]

        cst = sb("cst", [P, C_END])
        ident = cst[:, C_ID:C_ID + P]
        scan_keep = cst[:, C_SCAN:C_SCAN + T]
        level_mask = cst[:, C_MASK:C_MASK + 7 * CH].bitcast(I32).rearrange("p (l t) -> p l t", l=7)
        chunk_keep = cst[:, C_CHUNK:C_CHUNK + C5P]
        batch_rows = cst[:, C_BATCH:C_BATCH + NB]
        ones = sb("ones", [P, P])
        gains = sb("gains", [P, 6, KD])
        eps = sb("eps", [P, 1])
        one = sb("one", [P, 1])
        h = sb("h", [P, KD, T])
        Xs = alias("Xs", 2 * KD * T)
        xh = sb("xh", [P, KD, T], F32R)
        xl = sb("xl", [P, KD, T], F32R)
        Hs = alias("Hs", 2 * KD * T)
        yh = sb("yh", [P, KD, T], F32R)
        yl = sb("yl", [P, KD, T], F32R)
        raw = sb("raw", [P, 2, KD * P])
        wh = sb("wh", [P, 2, KD * P], F32R)
        wl = sb("wl", [P, 2, KD * P], F32R)
        acc = sb("acc", [P, NT * P])
        sq = sb("sq", [P, 2, T])
        R = sb("R", [P, T])
        gs = sb("gs", [P, T])
        us = sb("us", [P, T])
        act = sb("act", [P, T])
        rv = sb("rv", [P, 4, 20])
        diag = sb("diag", [P, 2, P])
        mst = sb("mst", [P, 4])
        AR = sb("AR", [P, 16 * T + MW])
        PR = AR[:, 0:16 * T].rearrange("p (f t) -> p f t", t=T)
        MM = AR[:, 16 * T:16 * T + MW]

        def view(base, at, *dims):
            n = 1
            for d in dims:
                n *= d
            v = base[:, at:at + n]
            if len(dims) == 1:
                return v
            names = "abcd"[:len(dims)]
            return v.rearrange(f"p ({' '.join(names)}) -> p {' '.join(names)}",
                               **{k: d for k, d in zip(names[1:], dims[1:])})

        PS = ctx.enter_context(nc.psum_tensor("PS", [P, 8, 512], F32))

        def bank(b, *dims, at=0, rows=P):
            n = 1
            for d in dims:
                n *= d
            v = PS[0:rows, :, :].rearrange("p b n -> p (b n)")[:, b * 512 + at:b * 512 + at + n]
            if len(dims) == 1:
                return v
            names = "abcd"[:len(dims)]
            return v.rearrange(f"p ({' '.join(names)}) -> p {' '.join(names)}",
                               **{k: d for k, d in zip(names[1:], dims[1:])})

        zb = view(MM, 0, 2, T)
        ge = view(MM, 1152, 2, T)
        gq = view(MM, 2304, 2, T)
        gk = view(MM, 3456, 2, T)
        vtok = view(MM, 4608, NT, H * DV)
        zg = gs[:]
        zt = view(MM, 7744, 2, T)
        wgate = view(MM, 8896, H * DK)
        bgate = view(MM, 9152, 2)
        ggla = view(MM, 9154, 1)
        wzg = view(MM, 9168, KD, RANK)
        Sall = view(Xs, 0, 2, NCH + 1, DV)
        S0 = view(Xs, 2304, 2, NB, DV)
        SC = view(Xs, 4352, H, NT, P)
        ktok = view(Xs, 6912, NT, 2 * P)
        kem = AR[0:TS, 4 * T:4 * T + NB * 2 * P].rearrange("p (b k) -> p b k", b=NB)
        oT = PR[:, 4:8, :]
        CA = view(MM, 0, G, L5 + 1, P5)
        tc = view(MM, 4608, G, C5P)
        sg = view(MM, 6656, G, C5P)
        sm = view(MM, 9296, 15, G)
        x0 = view(MM, 9776, NB, G)
        s1 = view(MM, 10032, NB, G)
        bglu = view(MM, 10288, 4)
        Win = view(Hs, 0, G, P)
        TT = view(Hs, 4096, G, P)
        bU, bV, BV, Bb = (view(AR, 512 * i, G, P5) for i in range(4))
        cU, cV = (view(AR, 2048 + 512 * i, G, P5) for i in range(2))
        pr, pi = (view(AR, 3072 + 288 * i, G, L5 + 1) for i in range(2))
        prr, pir = (view(AR, 3648 + 256 * i, G, L5) for i in range(2))
        x0s = view(AR, 4160, NB, G)
        dd = AR[0:P5, 4416:4416 + G]
        prep = AR[:, 4448:5120]
        WT = view(AR, 5120, G, L5, P5)
        Kt = AR[0:P5, 5120:9216].rearrange("p (g j) -> p g j", g=G)
        ktmp = AR[0:P5, 0:G * P5].rearrange("p (g q) -> p g q", g=G)
        nat = view(MM, 5120, 4, P)
        nat2 = view(MM, 5632, 4, P)
        x0n = view(MM, 6144, 2, P)
        x0sn = view(MM, 6400, 2, P)
        u2 = view(Xs, 0, G, C5)
        SF = Xs[:, 2304:6400]
        UT = SF[0:C5, :].rearrange("p (g s q) -> p g s q", g=G, s=L5)
        zin = view(SF, 0, G, C5P)
        zz = view(SF, 2048, G, C5P)
        Y2 = SF[0:C5, :].rearrange("p (t j) -> p t j", t=L5)
        SG = Xs[:, 6400:8704]
        XS = view(SG, 0, G, C5)
        keep5 = view(SG, 0, G, C5P)
        wglu = view(Xs, 8704, 4, P)
        zT = view(MM, 4608, 4, T)
        sig = view(MM, 6912, T)
        og = view(MM, 7488, T)
        s1o = view(AR, 12 * T, 3, P)
        Snew = view(AR, 12 * T, 2, NB, DV)
        SCp = view(MM, 9600, H, 4, CH)
        SCs = view(Xs, 8192, H, CH)
        osq = (gs[:], ge[:, 0, :], gk[:, 0, :], zt[:, 0, :])
        KVT = view(MM, 0, 16, M)
        KVN = view(MM, 4096, 2, 2 * D)
        mh = yh[:, :, 0:M]
        ml = yl[:, :, 0:M]
        mnat = view(MM, 4096, 2, D)
        msq = view(MM, 6144, D)
        qT = PR[:, 0:8, :]
        PT = view(AR, 8 * T, H, 2, TP)
        KB = [view(Xs, 4096, 2, D), view(Xs, 6144, 2, D), view(MM, 0, 2, D), view(MM, 2048, 2, D)]
        KBT = view(MM, 8192, KD, M)
        pp = view(Xs, 0, H, M)
        att = view(Xs, 1024, 16)
        os = view(Xs, 1040, 2, M)
        qz = view(Xs, 2048, KD, NB, 4 * BT)
        PTz = view(MM, 4096, 2, H, NB, 4 * BT)
        yy = PR[:, 0:8, :]
        yo = view(MM, 0, 2, D)
        xin = view(MM, 0, NT, D)

        groups = []

        def add(kind, src, nblk, K, row0, cols, **kw):
            n0 = sum(g["n"] for g in groups)
            groups.append(dict(kind=kind, src=src, n=nblk, K=K, row0=row0, cols=cols, n0=n0, **kw))

        def ffn(which):
            f0 = 0
            for i, nf in enumerate(FGROUPS):
                add("gu", A[f"w_ffn{which}_gu"], 2 * nf, KD, 0, (f0 * P, F + f0 * P, P), f0=f0 + (which - 1) * FT)
                add("down", A[f"w_ffn{which}_down"], KD, nf, f0 * P, (0, P, 2 * P),
                    norm=(1 if which == 1 else 4) if i == 2 else None, half=True)
                f0 += nf

        ffn(1)
        add("proj", A["w_in"], 8, KD, 0, (0, P, 2 * P), f0=0, first=True)
        add("proj", A["w_in"], 8, KD, 0, (D + RANK, D + RANK + P, 2 * P), f0=8)
        add("down", A["w_out"], KD, KD, 0, (0, P, 2 * P), norm=2, half=False)
        add("kv", A["w_ckv"], 16, KD, 0, (0, P, 2 * P))
        add("q", A["w_cq"], KD, KD, 0, (0, P, 2 * P))
        add("down", A["w_co"], KD, KD, 0, (0, P, 2 * P), norm=3, half=False)
        ffn(2)
        W_IN, W_OUT, KV, W_Q, W_O, FFN2 = 6, 8, 9, 10, 11, 12
        gain_of = {0: G_FFN1, 1: G_MIX, 2: G_CROSS, 3: G_FFN2, 4: G_FINAL}

        s_load, s_const = S("s_load"), S("s_const")
        s_x, x_ev = S("s_x"), S("x_ev")
        raw_in = [S("raw_in0"), S("raw_in1")]
        w_hi = S("w_hi")
        w_lo = S("w_lo")
        mm_done = S("mm_done")
        ps_free = S("ps_free")
        sq_ready, acc_ready = S("sq_ready"), S("acc_ready")
        x_hi, x_lo = S("x_hi"), S("x_lo")
        acc_zero = S("acc_zero")
        ss, rt, dg, rb, r_ready = S("ss"), S("rt"), S("dg"), S("rb"), S("r_ready")
        g_scaled, g_act, u_scaled, hid, hid_hi, hid_lo = (S(n) for n in (
            "g_scaled", "g_act", "u_scaled", "hid", "hid_hi", "hid_lo"))
        gla_out, s5_out, kv_out = S("gla_out"), S("s5_out"), S("kv_out")
        y_out = [S("y_out0"), S("y_out1")]

        block = ctx.enter_context(nc.Block())

        class Mark:

            def __init__(self, eng):
                self.eng, self.n = eng, {}

            def __call__(self, ins, name, by=1):
                ins.then_inc(S(name), by)
                self.n[name] = self.n.get(name, 0) + by
                self.eng.wait_ge(S(name), self.n[name])

        def chunk(t, k):
            return t[:, bass.ds(k, 1), :].rearrange("p a t -> p (a t)")

        @block.sync
        def _(e):
            e.dma_start(cst[:], consts).then_inc(s_load, 16)
            with nc.allow_non_contiguous_dma(reason="gains, 4 KB each"):
                for i, name in enumerate(("g_ffn1", "g_mix", "g_cross", "g_ffn2", "g_final", "g_mem")):
                    g = A[name] if name == "g_final" else A[name][0]
                    e.dma_start(gains[:, i, :], g.rearrange("(k p) -> p k", p=P)).then_inc(s_load, 16)
            e.dma_start(xin[:, 0:4, :], A["x_prompt"][0].rearrange("(n p) d -> p n d", p=P)).then_inc(s_x, 16)
            e.dma_start(xin[0:TS, 4, :], A["x_sample"].rearrange("b t d -> (b t) d")).then_inc(s_x, 16)
            for g in groups:
                K, (c0, c1, step) = g["K"], g["cols"]
                src = g["src"][0, g["row0"]:g["row0"] + K * P, :].rearrange("(k p) n -> p k n", p=P)

                def load(i):
                    for par in range(2):
                        e.wait_ge(w_lo, i * 2 + (g["n0"] + par + 1))
                        e.dma_start(raw[:, par, 0:K * P].rearrange("p (k n) -> p k n", k=K),
                                    src[:, :, bass.ds(i * step + (c0, c1)[par], P)]).then_inc(raw_in[par], 16)

                first = 0
                if g is groups[W_O]:
                    first = 1
                    load(0)
                    for n in range(2 * NB):
                        if n < 2:
                            e.wait_ge(mm_done, groups[W_O]["n0"] + 2)
                        elif n < 4:
                            e.wait_ge(S("s_mm"), 4)
                        elif n < 4 + NB:
                            e.wait_ge(S("kbt_mm"), 2 * (n - 4) + 2)
                        else:
                            e.wait_ge(S("pvs_mm"), n - 4 - NB + 1)
                        kv_src = A["cache_mem_k" if n < NB else "cache_mem_v"][0, n % NB]
                        e.dma_start(KB[n % 4], kv_src.rearrange("(j p) h d -> p j (h d)", p=P)).then_inc(S(f"kb_in{n % 4}"), 16)
                with e.Fori(first, g["n"] // 2) as i:
                    load(i)

        @block.gpsimd
        def _(e):
            e.memset(ones[:], 1.0).then_inc(s_const, 1)
            e.memset(eps[:], EPS).then_inc(s_const, 1)
            e.memset(one[:], 1.0).then_inc(s_const, 1)
            e.memset(acc[:, T:], 0.0).then_inc(s_const, 1)

            def sums(m):
                if m:
                    e.wait_ge(ss, m)
                    e.wait_ge(acc_ready, 8 * m)
                e.memset(acc[:, 0:T], 0.0).then_inc(acc_zero, 1)
                e.wait_ge(acc_zero, m + 1)
                for k in range(KD):
                    e.wait_ge(sq_ready, 8 * m + k + 1)
                    if 8 * m + k:
                        e.wait_ge(acc_ready, 8 * m + k)
                    e.tensor_tensor(acc[:, 0:T], acc[:, 0:T], sq[:, k % 2, :], ALU.add).then_inc(acc_ready, 1)

            mark = Mark(e)
            TTT, TSC = e.tensor_tensor, e.tensor_scalar

            def own(ins):
                mark(ins, "pool_own")

            def mul(o, a, b):
                own(TTT(o, a, b, ALU.mult))

            def poly(o, x, coeffs):
                own(TSC(o, x, coeffs[0], coeffs[1], ALU.mult, ALU.add))
                for c in coeffs[2:]:
                    mul(o, o, x)
                    own(TSC(o, o, c, None, ALU.add))

            def exp(o, x, k, pw):
                own(TSC(x, x, 88.0, -87.0, ALU.min, ALU.max))
                own(TSC(k, x, 1.4426950408889634, ROUND, ALU.mult, ALU.add))
                own(TSC(k, k, -ROUND, None, ALU.add))
                for part in (LN2_HI, LN2_LO):
                    own(TSC(pw, k, -part, None, ALU.mult))
                    own(TTT(x, x, pw, ALU.add))
                poly(o, x, [1.0 / math.factorial(i) for i in range(8, -1, -1)])
                own(TSC(k, k, 127.0, 8388608.0, ALU.add, ALU.mult))
                own(e.tensor_copy(pw.bitcast(I32), k))
                mul(o, o, pw)

            def times(o_r, o_i, a_r, a_i, b_r, b_i, u, v):
                mul(u, a_r, b_r)
                mul(v, a_i, b_i)
                own(TTT(o_r, u, v, ALU.subtract))
                mul(u, a_r, b_i)
                mul(v, a_i, b_r)
                own(TTT(o_i, u, v, ALU.add))

            def one_col(t, j):
                return t[:, :, j:j + 1].rearrange("p g a -> p (g a)")

            def wide(t, n):
                return t[:, :, None].broadcast_to([P, G, n])

            def s5_parameters():
                dt, dr, th, mag, r8, sn, cs, lr, li, t0, t1, t2, fr, fi = (sm[:, i, :] for i in range(14))
                e.wait_ge(S("prep_in"), 8)
                e.wait_ge(S("d_s5"), 16 * 12)
                exp(t0, dt, t1, t2)
                own(e.tensor_copy(dt, t0))
                mul(dr, dt, lr)
                mul(th, dt, li)
                own(TSC(t1, th, 1.0 / TWO_PI, None, ALU.mult))
                own(TSC(t1, t1, ROUND, None, ALU.add))
                own(TSC(t1, t1, -ROUND, None, ALU.add))
                for part in (PI_A, PI_B, PI_C):
                    own(TSC(t0, t1, -part, None, ALU.mult))
                    own(TTT(th, th, t0, ALU.add))
                own(TSC(th, th, 0.5, None, ALU.mult))
                exp(mag, dr, t1, t2)
                mul(r8, mag, mag)
                mul(r8, r8, r8)
                mul(r8, r8, r8)
                mul(t0, th, th)
                poly(t1, t0, [(-1.0) ** i / math.factorial(2 * i + 1) for i in range(7, -1, -1)])
                mul(t1, t1, th)
                poly(t2, t0, [(-1.0) ** i / math.factorial(2 * i) for i in range(8, -1, -1)])
                mul(sn, t1, t2)
                own(TSC(sn, sn, 2.0, None, ALU.mult))
                mul(cs, t1, t1)
                own(TSC(cs, cs, -2.0, 1.0, ALU.mult, ALU.add))
                own(e.memset(pr[:, :, 0:1], 1.0))
                own(e.memset(pi[:, :, 0:1], 0.0))
                ar, ai = one_col(pr, 1), one_col(pi, 1)
                mul(ar, mag, cs)
                mul(ai, mag, sn)
                own(TSC(t1, ar, -1.0, None, ALU.add))
                mul(fr, t1, lr)
                mul(t2, ai, li)
                own(TTT(fr, fr, t2, ALU.add))
                mul(fr, fr, sm[:, 14, :])
                mul(fi, ai, lr)
                mul(t2, t1, li)
                own(TTT(fi, fi, t2, ALU.subtract))
                mul(fi, fi, sm[:, 14, :])
                for w in (1, 2, 4):
                    times(pr[:, :, w + 1:2 * w + 1], pi[:, :, w + 1:2 * w + 1], pr[:, :, 1:w + 1], pi[:, :, 1:w + 1],
                          pr[:, :, w:w + 1].broadcast_to([P, G, w]), pi[:, :, w:w + 1].broadcast_to([P, G, w]),
                          view(prep, 0, G, w), view(prep, 256, G, w))
                for d, src in ((prr, pr), (pir, pi)):
                    own(e.tensor_copy(d, src[:, :, 0:L5][:, :, ::-1]))
                own(TSC(bV[0:64], bV[0:64], -1.0, None, ALU.mult))
                tb = view(prep, 0, G, P5)
                mul(Bb, bU, wide(fr, P5))
                mul(tb, bV, wide(fi, P5))
                own(TTT(Bb, Bb, tb, ALU.add))
                mul(BV, bV, wide(fr, P5))
                mul(tb, bU, wide(fi, P5))
                own(TTT(BV, BV, tb, ALU.subtract))
                for out, U, V, p_r, p_i, n, name in ((WT, Bb, BV, prr, pir, L5, "wt_ok"), (CA, cU, cV, pr, pi, L5 + 1, "ca_ok")):
                    for g in range(0, G, 8):
                        gg = slice(g, g + 8)
                        tv = view(AR, 0, 8, n, P5)

                        def over_j(t):
                            return t[:, gg, None, :].broadcast_to([P, 8, n, P5])

                        def over_q(t):
                            return t[:, gg, :][:, :, :, None].broadcast_to([P, 8, n, P5])

                        mul(out[:, gg], over_j(U), over_q(p_r))
                        mul(tv, over_j(V), over_q(p_i))
                        own(TTT(out[:, gg], out[:, gg], tv, ALU.add))
                    e.sem_inc(S(name), 1)
                a8r, a8i = one_col(pr, 8), one_col(pi, 8)
                t8 = view(prep, 0, NB, G)
                mul(s1, x0, a8r[:, None, :].broadcast_to([P, NB, G]))
                mul(t8, x0s, a8i[:, None, :].broadcast_to([P, NB, G]))
                own(TTT(s1[0:64], s1[0:64], t8[0:64], ALU.subtract))
                own(TTT(s1[64:128], s1[64:128], t8[64:128], ALU.add))
                def double():
                    times(t0, t1, cs, sn, cs, sn, t2, dr)
                    mul(t2, t0, t0)
                    mul(dr, t1, t1)
                    own(TTT(t2, t2, dr, ALU.add))
                    own(TSC(t2, t2, -0.5, 1.5, ALU.mult, ALU.add))
                    mul(cs, t0, t2)
                    mul(sn, t1, t2)

                for _ in range(3):
                    double()
                own(e.memset(tc[:, :, 0:1], 1.0))
                own(e.memset(sg[:, :, 0:1], 0.0))
                for w in (1, 2, 4, 8, 16, 32):
                    times(tc[:, :, w:2 * w], sg[:, :, w:2 * w], tc[:, :, 0:w], sg[:, :, 0:w], wide(cs, w), wide(sn, w),
                          view(AR, 0, G, w), view(AR, 2048, G, w))
                    if w < 32:
                        double()
                own(TSC(sg[64:128], sg[64:128], -1.0, None, ALU.mult))
                e.sem_inc(S("tables_ok"), 1)
            sums(0)
            s5_parameters()
            sums(1)
            e.wait_ge(mm_done, groups[W_IN]["n0"] + 2)
            e.memset(TT, 0.0).then_inc(S("tt_zero"), 1)
            e.wait_ge(mm_done, groups[W_OUT]["n0"] + 2)
            e.memset(wglu, 0.0).then_inc(S("tt_zero"), 1)
            e.wait_ge(S("mix_ok"), 4)
            e.wait_ge(S("zt_mm"), L5)
            e.wait_ge(S("s1_mm"), 1)
            e.wait_ge(S("glu_mm"), 4)
            e.memset(SC, 0.0).then_inc(S("sc_zero"), 1)
            e.memset(SCp, 0.0).then_inc(S("sc_zero"), 1)
            e.memset(SCs, 0.0).then_inc(S("sc_zero"), 1)
            e.wait_ge(S("sc_zero"), 3)
            e.memset(vtok[TS:P, NT - 1, :], 0.0).then_inc(S("sc_zero"), 1)
            e.wait_ge(S("sc_zero"), 4)
            e.memset(Sall[:, :, 0, :], 0.0).then_inc(S("sc_zero"), 1)
            sums(2)
            e.wait_ge(mm_done, groups[W_O]["n0"] + 2)
            mark(e.memset(qz, 0.0), "qz_own")
            e.wait_ge(ps_free, groups[W_O]["n0"] + 2)
            for c in range(4):
                e.tensor_copy(qz[:, :, c::4, BT * c:BT * c + BT],
                              qT[:, :, TP:T].rearrange("p f (b t) -> p f b t", b=NB)[:, :, c::4, :]).then_inc(S("qz_ok"), 1)
            e.wait_ge(S("pv_mm"), 8)
            e.wait_ge(kv_out, 64)
            e.memset(PTz, 0.0).then_inc(S("ptz_zero"), 1)
            sums(3)
            sums(4)

        @block.tensor
        def _(e):
            mark = Mark(e)

            def mm(out, lhsT, rhs, start=True, stop=True, **kw):
                return e.matmul(out, lhsT, rhs, start=start, stop=stop, **kw)

            def dense(n, par, K, xa, xb, width=TH, parts=2):
                e.wait_ge(w_lo, n + 3)
                e.wait_ge(ps_free, n + 1)
                last = None
                for k in range(K):
                    for wi, (w, x) in enumerate(((wh, xa), (wh, xb), (wl, xa))):
                        for j in range(parts):
                            last = mm(bank(2 * par + j, width), w[:, par, k * P:(k + 1) * P],
                                      x[:, k, j * width:(j + 1) * width],
                                      start=(k == 0 and wi == 0), stop=(k == K - 1 and wi == 2))
                last.then_inc(mm_done, 1)

            def dense_group(gi, xa, xb, **kw):
                g = groups[gi]
                with e.Fori(0, g["n"] // 2) as i:
                    for par in range(2):
                        dense(i * 2 + (g["n0"] + par), par, g["K"], xa, xb, **kw)

            def rms(m, cols=NT, src=acc):
                for j in range(NT):
                    last = mm(bank(7, 1, at=j), acc[:, j * P:(j + 1) * P], ones[:, 0:1])
                last.then_inc(ss, 1)
                for j in range(NT):
                    e.wait_ge(dg, m * NT + j + 1)
                    w = min(P, T - j * P)
                    last = mm(bank(4, w, at=j * P), ones[:], diag[:, j % 2, 0:w])
                    last.then_inc(rb, 1)

            e.wait_ge(s_load, 7 * 16)
            e.wait_ge(s_const, 4)
            e.wait_ge(s_x, 32)
            for k in range(KD):
                if k >= 2:
                    e.wait_ge(x_ev, k - 1)
                for j in range(NT):
                    w = min(P, T - j * P)
                    last = e.transpose(bank(4 + 2 * (k % 2), w, at=j * P), xin[0:w, j, k * P:(k + 1) * P],
                                       ident[0:w, 0:w])
                last.then_inc(S("x_tr"), 1)

            def s5_turn():
                e.wait_ge(S("d_s5"), 16 * 12)
                e.transpose(bank(4, G), nat2[0:G, 0, :], ident[0:G, 0:G])
                e.transpose(bank(4, G, at=G), nat2[0:G, 1, :], ident[0:G, 0:G]).then_inc(S("lam_mm"), 1)
                for j in range(4):
                    last = e.transpose(bank(5, P, at=j * P), nat[:, j, :], ident)
                last.then_inc(S("c_mm"), 1)
                e.wait_ge(S("x0n_in"), 64)
                for j in range(2):
                    e.transpose(bank(6, P, at=j * P), x0n[:, j, :], ident)
                    last = e.transpose(bank(6, P, at=256 + j * P), x0sn[:, j, :], ident)
                last.then_inc(S("x0_mm"), 1)

            def s5_matrices():
                e.wait_ge(S("wt_ok"), 1)
                for r in range(8):
                    if r >= 2:
                        e.wait_ge(S("win_ok"), r - 1)
                    for j in range(4):
                        last = e.transpose(bank(4 + r % 2, P, at=j * P), WT[:, 4 * r + j, :, :].rearrange("p s q -> p (s q)"), ident)
                    last.then_inc(S("win_mm"), 1)
                e.wait_ge(S("ca_ok"), 1)
                for r in range(8):
                    if r >= 2:
                        e.wait_ge(S("kt_ok"), r - 1)
                    for j in range(4):
                        g = 4 * r + j
                        last = mm(bank(6 + r % 2, P, at=j * P, rows=P5), Bb[:, g, :],
                                  CA[:, g, 0:L5, :].rearrange("p j q -> p (j q)"))
                    last.then_inc(S("kt_mm"), 1)
                e.wait_ge(S("win_ok"), 8)
                e.wait_ge(S("kt_ok"), 8)

            def ffn_pe(first, m):
                e.wait_ge(x_lo, 8 * (m + 1))
                e.wait_ge(acc_ready, 8 * (m + 1))
                rms(m)
                done = groups[first]["f0"]
                for i, nf in enumerate(FGROUPS):
                    dense_group(first + 2 * i, xh, xl)
                    if first == 0 and i == 0:
                        s5_turn()
                    done += nf
                    e.wait_ge(hid_lo, done)
                    dense_group(first + 2 * i + 1, yh, yl)

            ffn_pe(0, 0)
            s5_matrices()
            e.wait_ge(x_lo, 16)
            e.wait_ge(acc_ready, 16)
            rms(1)
            dense_group(W_IN, xh, xl)
            dense_group(W_IN + 1, xh, xl)
            e.wait_ge(S("wzg_ok"), 1)
            for k in range(KD):
                for j in range(2):
                    last = mm(bank(6 + j, TH, rows=RANK), wzg[:, k, :], h[:, k, j * TH:(j + 1) * TH],
                              start=k == 0, stop=k == KD - 1)
            last.then_inc(S("zg_mm"), 1)
            e.wait_ge(ps_free, groups[W_OUT]["n0"] + 2)
            for s in range(L5):
                if s >= 2:
                    e.wait_ge(S("ut_ok"), s - 1)
                for j in range(4):
                    last = e.transpose(bank(s % 2, P, at=j * P, rows=C5), PR[:, 12 + j, s::L5], ident)
                last.then_inc(S("ut_mm"), 1)
            e.wait_ge(S("ut_ok"), L5)
            for r in range(5):
                if r >= 2:
                    e.wait_ge(S("u2_ok"), r - 1)
                for j in range(7 * r, min(G, 7 * r + 7)):
                    last = e.transpose(bank(2 + r % 2, C5, at=(j % 7) * C5),
                                       UT[:, j, :, :].rearrange("p s q -> p (s q)"), ident[0:C5, 0:C5])
                last.then_inc(S("u2_mm"), 1)
            e.wait_ge(S("zg_ok"), 1)
            e.wait_ge(S("u2_ok"), 5)
            for r in range(5):
                if r >= 2:
                    e.wait_ge(S("d_ok"), r - 1)
                for j in range(7 * r, min(G, 7 * r + 7)):
                    at = (j % 7) * C5
                    mm(bank(4 + 2 * (r % 2), C5, at=at), Win[:, j, :], u2[:, j, :])
                    mm(PS[0:64, 5 + 2 * (r % 2), at:at + C5], Win[:, j, 64:128], u2[:, j, :])
                    last = mm(PS[64:128, 5 + 2 * (r % 2), at:at + C5], Win[:, j, 0:64], u2[:, j, :])
                last.then_inc(S("d_mm"), 1)
            e.wait_ge(S("xs_ok"), 1)
            e.wait_ge(S("tt_in"), 16 * L5)
            for r in range(8):
                if r >= 2:
                    e.wait_ge(S("y_g"), 2 * (r - 1))
                for j in range(4):
                    g = 4 * r + j
                    mm(bank(r % 2, P, at=j * P, rows=C5), u2[:, g, :], TT[:, g, :], stop=False)
                    last = mm(bank(r % 2, P, at=j * P, rows=C5), XS[:, g, :],
                              CA[:, g, 1:, :].rearrange("p j q -> p (j q)"), start=False)
                last.then_inc(S("y_mm"), 1)
            e.wait_ge(S("s1_ok"), 1)
            e.transpose(bank(2, P), s1[:, 0:4, :].rearrange("p b g -> p (b g)"), ident)
            e.transpose(bank(2, P, at=P), s1[:, 4:8, :].rearrange("p b g -> p (b g)"), ident)
            e.transpose(bank(2, P, at=2 * P, rows=G), sm[:, 14, :], ident).then_inc(S("s1_mm"), 1)
            e.wait_ge(S("y_g"), 16)
            for s in range(L5):
                if s >= 2:
                    e.wait_ge(S("zt_ok"), s - 1)
                for j in range(4):
                    last = e.transpose(bank(4 + s % 2, C5, at=j * C5), Y2[:, s, j * P:(j + 1) * P], ident[0:C5, 0:C5])
                last.then_inc(S("zt_mm"), 1)
            e.wait_ge(S("zt_ok"), L5)
            e.wait_ge(S("glu_in"), 16 * 9)
            for f in range(4):
                if f >= 2:
                    e.wait_ge(S("sig_ok"), f - 1)
                for j in range(2):
                    last = mm(bank(2 * (f % 2) + j, TH), wglu[:, f, :], zT[:, f, j * TH:(j + 1) * TH])
                last.then_inc(S("glu_mm"), 1)
            e.wait_ge(S("zg_ok"), 1)
            e.wait_ge(S("sig_ok"), 4)
            e.wait_ge(S("s1o_ok"), 1)
            e.wait_ge(S("d_gla"), 16 * 3)
            for i in range(2):
                for j in range(2):
                    last = mm(bank(2 * i + j, TH), wgate[0:RANK, i * P:(i + 1) * P], zg[0:RANK, j * TH:(j + 1) * TH])
            last.then_inc(S("z_mm"), 1)
            e.wait_ge(S("zg_ok"), 1)
            for j in range(NT):
                if j >= 2:
                    e.wait_ge(S("vtok_ok"), j - 1)
                w = min(P, T - j * P)
                for f in range(4):
                    last = e.transpose(bank(6 + j % 2, P, at=f * P, rows=w), PR[:, 4 + f, j * P:j * P + w], ident)
                last.then_inc(S("vtok_mm"), 1)
            e.wait_ge(S("ke_ok"), 1)
            e.wait_ge(S("vtok_ok"), NT)
            for j in range(NT):
                if j >= 2:
                    e.wait_ge(S("ktok_ok"), j - 1)
                w = min(P, T - j * P)
                for f in range(2):
                    last = e.transpose(bank(6 + j % 2, P, at=f * P, rows=w), gk[:, f, j * P:j * P + w], ident)
                last.then_inc(S("ktok_mm"), 1)
            rounds = [(0, PR[:, 0:2, :], PR[:, 2:4, :])] + [(lv + 1, gq, gk) for lv in range(len(LEVELS))]
            for r, qq, kk in rounds:
                if r:
                    e.wait_ge(S("lev_in"), r)
                    e.wait_ge(S("lev_ok"), r)
                nch = NCH + 1 if r <= 3 else NCH
                for c in range(nch):
                    for hd in range(H):
                        a, f = (hd % 2) * DK, hd // 2
                        o0 = (c % 2) * CH
                        last = mm(PS[o0:o0 + CH, hd, (c // 2) * CH:(c // 2 + 1) * CH],
                                  kk[a:a + DK, f, c * CH:(c + 1) * CH], qq[a:a + DK, f, c * CH:(c + 1) * CH])
                last.then_inc(S("lev_mm"), 1)
            e.wait_ge(S("ktok_ok"), NT)
            e.wait_ge(S("kem_ok"), 1)
            for c in range(NCH):
                for hd in range(H):
                    a, f = (hd % 2) * DK, hd // 2
                    o0 = (c % 2) * CH
                    last = mm(PS[a:a + DK, 4 + 2 * f + c % 2, (c // 2) * DV:(c // 2 + 1) * DV],
                              ktok[o0:o0 + CH, c // 2, hd * DK:(hd + 1) * DK],
                              vtok[o0:o0 + CH, c // 2, hd * DV:(hd + 1) * DV])
            last.then_inc(S("kv_mm"), 1)
            e.wait_ge(S("lev_ok"), 7)
            for b in range(NB):
                for hd in range(H):
                    a, f = (hd % 2) * DK, hd // 2
                    last = mm(PS[a:a + DK, 2 * f + b // 4, (b % 4) * DV:(b % 4 + 1) * DV],
                              kem[:, b, hd * DK:(hd + 1) * DK], vtok[0:TS, 4, hd * DV:(hd + 1) * DV])
            last.then_inc(S("kvs_mm"), 1)
            e.wait_ge(S("qe_ok"), 1)
            e.wait_ge(S("st_ok"), 1)
            e.wait_ge(S("sts_ok"), 1)
            e.wait_ge(S("sc_ok"), 1)
            for f in range(2):
                for hh in range(2):
                    hd, a = 2 * f + hh, hh * DK
                    B = 4 * f + 2 * hh
                    for c in range(1, NCH):
                        mm(bank(B, CH, at=c * CH), Sall[a:a + DK, f, c, :], gq[a:a + DK, f, c * CH:(c + 1) * CH],
                           start=(c == 1), stop=False, skip_group_check=True)
                    for b in range(NB):
                        t0 = TP + b * BT
                        mm(bank(B, BT, at=t0), S0[a:a + DK, f, b, :], gq[a:a + DK, f, t0:t0 + BT],
                           start=(b == 0), stop=False, skip_group_check=True)
                    for j in range(NT):
                        w = min(P, T - j * P)
                        last = mm(bank(B, w, at=j * P), vtok[:, j, hd * DV:(hd + 1) * DV], SC[:, hd, j, 0:w],
                                  start=False, stop=True, skip_group_check=True)
                    last.then_inc(S("o_mm"), 1)
            e.wait_ge(S("osq_ok"), 4)
            e.wait_ge(S("oss_zero"), 1)
            for hd in range(H):
                for j in range(NT):
                    w = min(P, T - j * P)
                    last = mm(bank(0, 1, at=hd * NT + j, rows=w), osq[hd][:, j * P:j * P + w], ones[:, 0:1])
            last.then_inc(S("oss_mm"), 1)
            for hd in range(H):
                if hd >= 2:
                    e.wait_ge(S("orr_ok"), hd - 1)
                for j in range(NT):
                    q = hd * NT + j
                    e.wait_ge(S("odg"), q + 1)
                    w = min(P, T - j * P)
                    last = mm(bank(2 + 2 * (hd % 2), w, at=j * P), ones[0:w, :], diag[0:w, q % 2, 0:w])
                    last.then_inc(S("orb"), 1)
            e.wait_ge(S("mix_ok"), 8)
            dense_group(W_OUT, yh, yl)
            e.wait_ge(S("mem_ok"), 2)
            e.wait_ge(mm_done, groups[KV]["n0"] + 2)
            for k in range(KD):
                if k >= 2:
                    e.wait_ge(S("memx_lo"), k - 1)
                for j in range(2):
                    last = e.transpose(bank(4 + k % 2, P, at=j * P), mnat[:, j, k * P:(k + 1) * P], ident)
                last.then_inc(S("memt_mm"), 1)
            e.wait_ge(S("memx_lo"), KD)
            dense_group(KV, yh, yl, width=M, parts=1)
            e.wait_ge(ps_free, groups[W_Q]["n0"] + 2)
            for r in range(8):
                if r >= 2:
                    e.wait_ge(S("nat_ok"), r - 1)
                for j in range(4):
                    last = e.transpose(bank(4 + r % 2, P, at=j * P), KVT[:, 4 * (r % 4) + j, (r // 4) * P:(r // 4 + 1) * P], ident)
                last.then_inc(S("nat_mm"), 1)
            e.wait_ge(S("nat_ok"), 8)
            e.wait_ge(x_lo, 24)
            e.wait_ge(acc_ready, 24)
            rms(2)
            dense_group(W_Q, xh, xl)
            e.wait_ge(ps_free, groups[W_O]["n0"] + 2)
            for j in range(4):
                for hd in range(H):
                    for f in range(2):
                        last = mm(bank(4, M, at=hd * M), qT[:, 2 * hd + f, j * P:(j + 1) * P], KVT[:, 2 * hd + f, :],
                                  start=f == 0, stop=f == 1)
                last.then_inc(S("s_mm"), 1)
                e.wait_ge(S("p_ok"), j + 1)
                for hd in range(H):
                    for f in range(2):
                        last = e.transpose(bank(6, P, at=(2 * hd + f) * P), pp[:, hd, f * P:(f + 1) * P], ident)
                last.then_inc(S("pt_mm"), 1)
            e.wait_ge(S("pt_ok"), 4)
            for f in range(8):
                if f >= 2:
                    e.wait_ge(S("pv_lo"), f - 1)
                for j in range(2):
                    last = mm(bank(4 + f % 2, TP), KVN[:, j, D + f * P:D + (f + 1) * P], PT[:, f // 2, j, :],
                              start=j == 0, stop=j == 1)
                last.then_inc(S("pv_mm"), 1)
            def turn_keys(b, half):
                if b:
                    e.wait_ge(S(("kbt_a", "kbt_v")[half]), b)
                for f in range(4 * half, 4 * half + 4):
                    for j in range(2):
                        last = e.transpose(bank(0, P, at=f * M + j * P), KB[b % 4][:, j, f * P:(f + 1) * P], ident)
                last.then_inc(S("kbt_mm"), 1)

            def turn_probs(c):
                e.wait_ge(S("p_ok"), 5 + c)
                for j in range(2):
                    last = e.transpose(bank(4 + c, P, at=j * P), pp[:, c, j * P:(j + 1) * P], ident)
                last.then_inc(S("pt_mm"), 1)

            e.wait_ge(S("pv_lo"), 8)
            e.wait_ge(S("kb_in0"), 16)
            turn_keys(0, 0)
            turn_keys(0, 1)
            e.wait_ge(S("qz_ok"), 4)
            for b in range(NB):
                for half in range(2):
                    e.wait_ge(S(("kbt_a", "kbt_v")[half]), b + 1)
                    for hd in (2 * half, 2 * half + 1):
                        for f in range(2):
                            last = mm(PS[32 * hd:32 * hd + 32, 6 + b // 4, 0:M], qz[:, 2 * hd + f, b, :],
                                      KBT[:, 2 * hd + f, :], start=(b % 4 == 0 and f == 0), stop=(b % 4 == 3 and f == 1),
                                      skip_group_check=True)
                    last.then_inc(S("ssm_mm"), 1)
                    if b + 1 < NB:
                        if half == 0:
                            e.wait_ge(S(f"kb_in{(b + 1) % 4}"), 16 * ((b + 1) // 4 + 1))
                        turn_keys(b + 1, half)
                    elif half == 0:
                        turn_probs(0)
            for c in range(2):
                if c:
                    turn_probs(1)
                e.wait_ge(S("pt_ok"), 5 + c)
                for b in range(4 * c, 4 * c + 4):
                    e.wait_ge(S(f"kb_in{b % 4}"), 16 * (b // 4 + 3))
                    for hd in range(H):
                        for j in range(2):
                            last = mm(PS[32 * hd:32 * hd + 32, c, 0:CD], PTz[:, j, hd, b, :],
                                      KB[b % 4][:, j, hd * CD:(hd + 1) * CD], start=(b % 4 == 0 and j == 0),
                                      stop=(b % 4 == 3 and j == 1), skip_group_check=True)
                    last.then_inc(S("pvs_mm"), 1)
            for c in range(2):
                e.wait_ge(S("os_ok"), c + 1)
                for f in range(2):
                    last = e.transpose(bank(2 + c, P, at=f * P), os[:, c, f * P:(f + 1) * P], ident)
                last.then_inc(S("ost_mm"), 1)
            e.wait_ge(S("pvs_lo"), 2)
            dense_group(W_O, yh, yl)
            ffn_pe(FFN2, 3)
            e.wait_ge(acc_ready, 40)
            rms(4)
            for j in range(NT):
                e.wait_ge(S("yy_ok"), 8)
                if j >= 2:
                    e.wait_ge(S("yo_ok"), j - 1)
                w = min(P, T - j * P)
                for k in range(KD):
                    last = e.transpose(bank(2 * (j % 2), P, at=k * P, rows=w), yy[:, k, j * P:j * P + w], ident)
                last.then_inc(S("y_tr"), 1)

        @block.scalar
        def _(e):
            mark = Mark(e)

            def conv(gi, i, par):
                n0, K = groups[gi]["n0"], groups[gi]["K"]
                e.wait_ge(raw_in[par], i * 16 + (n0 // 2 * 16 + 16))
                e.wait_ge(mm_done, i * 2 + (n0 + par + 1))
                e.activation(wh[:, par, 0:K * P], raw[:, par, 0:K * P], ACT.Copy).then_inc(w_hi, 1)

            def group(gi, body):
                g = groups[gi]

                def step(i, last):
                    conv(gi, i, 1)
                    body(i, i * 2 + g["n0"], 0)
                    if not last:
                        conv(gi, i + 1, 0)
                    elif gi + 1 < len(groups):
                        conv(gi + 1, 0, 0)
                    body(i, i * 2 + (g["n0"] + 1), 1)

                with e.Fori(0, g["n"] // 2 - 1) as i:
                    step(i, False)
                step(g["n"] // 2 - 1, True)

            def norm_in(m, i, par):
                e.wait_ge(acc_ready, i * 2 + (8 * m + par - 1))
                k = i * 2 + par
                if m < 4:
                    e.activation(chunk(xh, k), chunk(h, k), ACT.Copy,
                                 scale=gains[:, gain_of[m], bass.ds(k, 1)]).then_inc(x_hi, 1)
                e.activation(sq[:, par, :], chunk(h, k), ACT.Square).then_inc(sq_ready, 1)

            def rms(m):
                e.wait_ge(ss, m + 1)
                e.activation(rv[:, 0, 0:NT], bank(7, NT), ACT.Sqrt, bias=eps[:], scale=1.0 / D).then_inc(rt, 1)

            def ffn(gi):
                for i in range(len(FGROUPS)):
                    g, d = groups[gi + 2 * i], groups[gi + 2 * i + 1]

                    def hidden(i, n, par, g=g):
                        if par == 0:
                            e.wait_ge(g_scaled, i + (g["f0"] + 1))
                            e.activation(act[:], gs[:], ACT.Silu).then_inc(g_act, 1)
                        else:
                            e.wait_ge(hid, i + (g["f0"] + 1))
                            e.activation(chunk(yh, i), us[:], ACT.Copy).then_inc(hid_hi, 1)

                    def down(i, n, par, d=d):
                        if d["norm"] is not None:
                            e.wait_ge(ps_free, n + 3)
                            norm_in(d["norm"], i, par)

                    group(gi + 2 * i, hidden)
                    group(gi + 2 * i + 1, down)

            def nothing(i, n, par):
                pass

            conv(0, 0, 0)
            e.wait_ge(s_load, 7 * 16)
            e.wait_ge(s_const, 4)
            for k in range(KD):
                e.wait_ge(x_ev, k + 1)
                e.activation(xh[:, k, :], h[:, k, :], ACT.Copy, scale=gains[:, G_FFN1, k:k + 1]).then_inc(x_hi, 1)
                if k >= 2:
                    e.wait_ge(acc_ready, k - 1)
                e.activation(sq[:, k % 2, :], h[:, k, :], ACT.Square).then_inc(sq_ready, 1)
            rms(0)
            with nc.allow_non_contiguous_dma(reason="16-column rows of w_in, small parameters"):
                e.dma_start(wzg, A["w_in"][0, :, D:D + RANK].rearrange("(k p) r -> p k r", p=P)).then_inc(S("wzg_in"), 16)
                e.dma_start(wgate[0:RANK, :], A["w_gla_gate"][0]).then_inc(S("d_gla"), 16)
                e.dma_start(bgate, A["b_gla_gate"][0].rearrange("(f p) -> p f", p=P)).then_inc(S("d_gla"), 16)
                e.dma_start(ggla, A["g_gla_out"][0].rearrange("(p a) -> p a", a=1)).then_inc(S("d_gla"), 16)
                for a in range(2):
                    e.dma_start(nat2[0:G, 0, a * 64:(a + 1) * 64], A["s5_lambda_re"][0]).then_inc(S("d_s5"), 16)
                    e.dma_start(nat2[0:G, 1, a * 64:(a + 1) * 64], A["s5_lambda_im"][0]).then_inc(S("d_s5"), 16)
                e.dma_start(sm[:, 0, :], A["s5_log_dt"].broadcast_to([P, G])).then_inc(S("d_s5"), 16)
                for a, nm in enumerate(("s5_b_re", "s5_b_im")):
                    src = A[nm][0].rearrange("g n p -> n g p")
                    e.dma_start(bU[64 * a:64 * a + 64], src).then_inc(S("d_s5"), 16)
                    e.dma_start(bV[64 * (1 - a):64 * (1 - a) + 64], src).then_inc(S("d_s5"), 16)
                    e.dma_start(nat[:, :, 64 * a:64 * a + 64],
                                A[("s5_c_re", "s5_c_im")[a]][0].rearrange("(j g) p n -> (g p) j n", j=4)).then_inc(S("d_s5"), 16)
                e.dma_start(dd, A["s5_d"][0].rearrange("g p -> p g")).then_inc(S("d_s5"), 16)
                for a, nm in enumerate(("state_s5_re", "state_s5_im")):
                    src = A[nm][0].rearrange("(j b) g n -> (b g) j n", j=2)
                    e.dma_start(x0n[:, :, 64 * a:64 * a + 64], src).then_inc(S("x0n_in"), 16)
                    e.dma_start(x0sn[:, :, 64 * (1 - a):64 * (1 - a) + 64], src).then_inc(S("x0n_in"), 16)
                e.dma_start(bglu, A["s5_b_glu"][0].rearrange("(j g) p -> (g p) j", j=4)).then_inc(S("glu_in"), 16)
            ffn(0)
            for r in range(8):
                e.wait_ge(S("win_mm"), r + 1)
                e.activation(Win[:, 4 * r:4 * r + 4, :], bank(4 + r % 2, 4, P), ACT.Copy).then_inc(S("win_ok"), 1)
            rms(1)
            group(W_IN, nothing)
            e.wait_ge(S("tt_zero"), 1)
            e.wait_ge(S("ktd_ok"), 1)
            for s in range(L5):
                e.dma_start(TT[P5 * s:P5 * s + P5, :, P5 * s:P], Kt[:, :, 0:P - P5 * s]).then_inc(S("tt_in"), 16)
            group(W_IN + 1, nothing)
            with nc.allow_non_contiguous_dma(reason="16 columns a row"):
                e.wait_ge(S("tt_zero"), 2)
                for gi in range(8):
                    e.dma_start(wglu[16 * gi:16 * gi + 16, :, 16 * gi:16 * gi + 16],
                                A["s5_w_glu"][0].rearrange("(j g) p q -> g p j q", j=4)[gi]).then_inc(S("glu_in"), 16)
            for s in range(L5):
                e.wait_ge(S("ut_mm"), s + 1)
                e.activation(UT[:, :, s, :], bank(s % 2, G, P5, rows=C5), ACT.Copy).then_inc(S("ut_ok"), 1)
            e.wait_ge(S("xs_ok"), 1)
            for r in range(8):
                e.wait_ge(S("y_mm"), r + 1)
                for t in range(2):
                    e.activation(Y2[:, 4 * t:4 * t + 4, 64 * r:64 * r + 64].rearrange("p t (g q) -> p g t q", g=4),
                                 bank(r % 2, 4, L5, P5, rows=C5)[:, :, 4 * t:4 * t + 4, :], ACT.Gelu_apprx_tanh).then_inc(S("y_g"), 1)
            for f in range(4):
                e.wait_ge(S("glu_mm"), f + 1)
                if f:
                    e.wait_ge(S("so_ok"), f)
                e.activation(sig.rearrange("p (a t) -> p a t", a=2), PS[:, 2 * (f % 2):2 * (f % 2) + 2, 0:TH], ACT.Sigmoid,
                             bias=bglu[:, f:f + 1]).then_inc(S("sig_ok"), 1)
                e.wait_ge(S("so_ok"), f + 1)
                e.activation(yh[:, 4 + f, :], og, ACT.Copy).then_inc(S("mix_hi"), 1)
            e.wait_ge(S("s1o_ok"), 1)
            for a, nm in enumerate(("re", "im")):
                for j in range(2):
                    e.dma_start(O[f"s5_{nm}_s"][0].rearrange("(j b) g n -> j (b g) n", j=2)[j],
                                s1o[:, j, 64 * a:64 * a + 64]).then_inc(s5_out, 16)
                e.dma_start(O[f"s5_{nm}_p"][0, 0], s1o[0:G, 2, 64 * a:64 * a + 64]).then_inc(s5_out, 16)
            e.wait_ge(S("sc_zero"), 5)
            for f in range(2):
                e.dma_start(S0[:, f, :, :], A["state_gla"][0, :, 2 * f:2 * f + 2].rearrange("b q d e -> (q d) b e")).then_inc(S("s0_in"), 16)
            e.wait_ge(S("z_sb"), 2)
            mark(e.activation(zt, zb, ACT.Abs), "act_own")
            mark(e.activation(zt, zt, ACT.Exp, scale=-1.0), "act_own")
            mark(e.activation(zt, zt, ACT.Ln, bias=one[:]), "ln_ok")
            for j in range(NT):
                w = min(P, T - j * P)
                e.wait_ge(S("vtok_mm"), j + 1)
                e.activation(vtok[0:w, j, :], bank(6 + j % 2, 512, rows=w), ACT.Copy).then_inc(S("vtok_ok"), 1)
            e.wait_ge(S("ke_rel"), 2)
            e.activation(ge, ge, ACT.Exp, scale=1.0 / TAU).then_inc(S("ke_exp"), 1)
            for j in range(NT):
                w = min(P, T - j * P)
                e.wait_ge(S("ktok_mm"), j + 1)
                e.activation(ktok[0:w, j, :], bank(6 + j % 2, 2 * P, rows=w), ACT.Copy).then_inc(S("ktok_ok"), 1)
            for lv, hs in enumerate(LEVELS):
                TL = T if hs <= 4 else TP
                e.wait_ge(S("rel_ok"), lv + 1)
                mark(e.activation(ge[:, :, 0:TL], ge[:, :, 0:TL], ACT.Abs), "act_own")
                e.activation(ge[:, :, 0:TL], ge[:, :, 0:TL], ACT.Exp, scale=-1.0 / TAU).then_inc(S("e_ok"), 1)
            e.wait_ge(S("lev_in"), len(LEVELS))
            e.activation(ge, zb, ACT.Exp, scale=1.0 / TAU).then_inc(S("eb_ok"), 1)
            for hd in range(H):
                e.wait_ge(S("o_sb"), hd + 1)
                e.wait_ge(S("o_mm"), H)
                e.activation(osq[hd], oT[:, hd, :], ACT.Square).then_inc(S("osq_ok"), 1)
            e.wait_ge(S("oss_mm"), 1)
            e.activation(rv[:, 0, :], bank(0, 20), ACT.Sqrt, bias=eps[:], scale=1.0 / DV).then_inc(S("ort"), 1)
            for hd in range(H):
                if hd:
                    e.wait_ge(S("og_ok"), hd)
                e.activation(act[:], PR[:, 8 + hd, :], ACT.Silu).then_inc(S("rs_ok"), 1)
                e.wait_ge(S("og_ok"), hd + 1)
                e.activation(yh[:, hd, :], us[:], ACT.Copy).then_inc(S("mix_hi"), 1)
            e.wait_ge(S("st_ok"), 1)
            e.wait_ge(S("snew_ok"), 1)
            for f in range(2):
                e.dma_start(O["gla_p"][0, 0, 2 * f:2 * f + 2].rearrange("q d e -> (q d) e"), Sall[:, f, NCH, :]).then_inc(gla_out, 16)
                e.dma_start(O["gla_s"][0, :, 2 * f:2 * f + 2].rearrange("b q d e -> (q d) b e"), Snew[:, f, :, :]).then_inc(gla_out, 16)
            e.wait_ge(gla_out, 64)
            e.wait_ge(S("oss_mm"), 1)
            e.dma_start(mnat, A["mem_prompt"][0].rearrange("(j p) d -> p j d", p=P)).then_inc(S("mem_in"), 16)

            def norm2(i, n, par):
                e.wait_ge(ps_free, n + 3)
                norm_in(2, i, par)

            group(W_OUT, norm2)
            e.wait_ge(S("mem_in"), 16)
            for j in range(2):
                mark(e.activation(msq, mnat[:, j, :], ACT.Square, accum_out=mst[:, j:j + 1]), "act_own")
            e.activation(mst[:, 2:4], mst[:, 0:2], ACT.Sqrt, bias=eps[:], scale=1.0 / D).then_inc(S("mrt"), 1)
            e.wait_ge(mm_done, groups[KV]["n0"] + 2)
            for k in range(KD):
                e.wait_ge(S("memt_mm"), k + 1)
                e.activation(mh[:, k, :], bank(4 + k % 2, M), ACT.Copy, scale=gains[:, G_MEM, k:k + 1]).then_inc(S("memx_hi"), 1)
            group(KV, nothing)
            e.wait_ge(S("nat_ok"), 8)
            for j in range(2):
                for a, nm in enumerate(("mem_k", "mem_v")):
                    e.dma_start(O[nm][0, 0, j * P:(j + 1) * P].rearrange("m h d -> m (h d)"),
                                KVN[:, j, a * D:(a + 1) * D]).then_inc(kv_out, 16)
            rms(2)
            group(W_Q, nothing)

            def softmax(r, w):
                e.wait_ge(S("mx_ok"), r + 1)
                if r:
                    e.wait_ge(S("pt_mm"), r)
                for hd in range(H):
                    e.activation(pp[0:w, hd, :], bank(4, H, M, rows=w)[:, hd, :], ACT.Exp, bias=att[0:w, 4 + hd:5 + hd],
                                 scale=CD ** -0.5, accum_out=att[0:w, 8 + hd:9 + hd]).then_inc(S("exp_ok"), 1)

            def softmax_decode(c):
                e.wait_ge(S("mx_ok"), 5 + c)
                e.activation(pp[:, c, :], bank(6 + c, M), ACT.Exp, bias=att[:, 4 + c:5 + c],
                             scale=CD ** -0.5, accum_out=att[:, 8 + c:9 + c]).then_inc(S("exp_ok"), 1)

            for r in range(4):
                softmax(r, P)
            for f in range(8):
                e.wait_ge(S("pv_mm"), f + 1)
                e.activation(yh[:, f, 0:TP], bank(4 + f % 2, TP), ACT.Copy).then_inc(S("pv_hi"), 1)
            e.wait_ge(kv_out, 64)
            for b in range(NB):
                e.wait_ge(S("kbt_mm"), 2 * b + 1)
                if b:
                    e.wait_ge(S("ssm_mm"), 2 * b - 1)
                e.activation(KBT[:, 0:4, :].rearrange("p f m -> p (f m)"), bank(0, 1024), ACT.Copy).then_inc(S("kbt_a"), 1)
                if b == 5:
                    softmax_decode(0)
            softmax_decode(1)
            for c in range(2):
                e.wait_ge(S("ost_mm"), c + 1)
                e.activation(yh[:, :, TP + 32 * c:TP + 32 * c + 32].rearrange("p (h f) t -> p f h t", f=2),
                             bank(2 + c, 2, H, 32), ACT.Copy).then_inc(S("pvs_hi"), 1)

            def norm3(i, n, par):
                e.wait_ge(ps_free, n + 3)
                norm_in(3, i, par)

            group(W_O, norm3)
            rms(3)
            ffn(FFN2)
            rms(4)
            for j in range(NT):
                w = min(P, T - j * P)
                e.wait_ge(S("yo_ok"), j + 1)
                dst = O["y_p"][0, j * P:(j + 1) * P, :] if j < 4 else O["y_s"].rearrange("b t d -> (b t) d")
                e.dma_start(dst, yo[0:w, j % 2, :]).then_inc(y_out[j % 2], 16)
            e.wait_ge(y_out[0], 16 * 3)
            e.wait_ge(y_out[1], 16 * 2)
            e.wait_ge(s5_out, 16 * 6)

        @block.vector
        def _(e):
            mark = Mark(e)
            TTT, TSC, STT, CP = e.tensor_tensor, e.tensor_scalar, e.scalar_tensor_tensor, e.tensor_copy

            def own(ins):
                mark(ins, "dve_own")

            def conv(gi, i, par):
                n0, K = groups[gi]["n0"], groups[gi]["K"]
                e.wait_ge(w_hi, i * 2 + (n0 + par + 1))
                TTT(wl[:, par, 0:K * P], raw[:, par, 0:K * P], wh[:, par, 0:K * P].bitcast(F32), ALU.subtract).then_inc(w_lo, 1)

            def group(gi, body):
                g = groups[gi]

                def step(i, last):
                    conv(gi, i, 1)
                    e.wait_ge(mm_done, i * 2 + (g["n0"] + 3))
                    body(i, i * 2 + g["n0"], 0)
                    if not last:
                        conv(gi, i + 1, 0)
                    elif gi + 1 < len(groups):
                        conv(gi + 1, 0, 0)
                    e.wait_ge(mm_done, i * 2 + (g["n0"] + 4))
                    body(i, i * 2 + (g["n0"] + 1), 1)

                with e.Fori(0, g["n"] // 2 - 1) as i:
                    step(i, False)
                step(g["n"] // 2 - 1, True)

            def halves(b):
                return PS[:, b:b + 2, 0:TH]

            def two(ap):
                return ap.rearrange("p (a t) -> p a t", a=2)

            def norm_in(m, i, par):
                k = i * 2 + par
                if m < 4:
                    e.wait_ge(x_hi, i * 2 + (8 * m + par + 1))
                    STT(chunk(xl, k), chunk(h, k), gains[:, gain_of[m], bass.ds(k, 1)], chunk(xh, k).bitcast(F32),
                        ALU.mult, ALU.subtract).then_inc(x_lo, 1)

            def inverse(n, width):
                own(e.reciprocal(rv[:, 2, 0:n], rv[:, 0, 0:n]))
                own(TTT(rv[:, 3, 0:n], rv[:, 2, 0:n], rv[:, 2, 0:n], ALU.mult))
                own(TTT(rv[:, 3, 0:n], rv[:, 3, 0:n], rv[:, 1, 0:n], ALU.mult))
                own(TSC(rv[:, 3, 0:n], rv[:, 3, 0:n], -0.5, 1.5, ALU.mult, ALU.add))
                own(TTT(rv[:, 3, 0:n], rv[:, 3, 0:n], rv[:, 2, 0:n], ALU.mult))

            def rms(m):
                e.wait_ge(rt, m + 1)
                own(TSC(rv[:, 1, 0:NT], bank(7, NT), 1.0 / D, EPS, ALU.mult, ALU.add))
                inverse(NT, D)
                for j in range(NT):
                    if m * NT + j >= 2:
                        e.wait_ge(rb, m * NT + j - 1)
                    TSC(diag[:, j % 2, :], ident, rv[:, 3, j:j + 1], None, ALU.mult).then_inc(dg, 1)
                e.wait_ge(rb, (m + 1) * NT)
                mark(CP(R[:], bank(4, T)), "r_ready")

            def down(g):
                def body(i, n, par):
                    k = i * 2 + par
                    hk = chunk(h, k)
                    STT(two(hk), halves(2 * par), 0.5 if g["half"] else 1.0, two(hk), ALU.mult, ALU.add).then_inc(ps_free, 1)
                    if g["norm"] is not None:
                        e.wait_ge(ps_free, n + 3)
                        norm_in(g["norm"], i, par)
                return body

            def ffn(gi):
                for i in range(len(FGROUPS)):
                    g = groups[gi + 2 * i]

                    def hidden(i, n, par, g=g):
                        if par == 0:
                            TTT(two(gs[:]), halves(0), two(R[:]), ALU.mult).then_inc(g_scaled, 1)
                            e.wait_ge(g_scaled, i + (g["f0"] + 1))
                            e.sem_inc(ps_free, 1)
                        else:
                            TTT(two(us[:]), halves(2), two(R[:]), ALU.mult).then_inc(ps_free, 1)
                            e.wait_ge(ps_free, n + 3)
                            e.wait_ge(g_act, i + (g["f0"] + 1))
                            TTT(us[:], us[:], act[:], ALU.mult).then_inc(hid, 1)
                            e.wait_ge(hid, i + (g["f0"] + 1))
                            e.wait_ge(hid_hi, i + (g["f0"] + 1))
                            TTT(chunk(yl, i), us[:], chunk(yh, i).bitcast(F32), ALU.subtract).then_inc(hid_lo, 1)

                    group(gi + 2 * i, hidden)
                    if gi == 0 and i == 0:
                        s5_turned()
                    group(gi + 2 * i + 1, down(groups[gi + 2 * i + 1]))

            def s5_turned():
                e.wait_ge(S("lam_mm"), 1)
                mark(CP(sm[:, 7:9, :], bank(4, 2, G)), "prep_in")
                own(TTT(sm[:, 12:14, :], sm[:, 7:9, :], sm[:, 7:9, :], ALU.mult))
                own(TTT(sm[:, 14, :], sm[:, 12, :], sm[:, 13, :], ALU.add))
                mark(e.reciprocal(sm[:, 14, :], sm[:, 14, :]), "prep_in")
                e.wait_ge(S("c_mm"), 1)
                cc = bank(5, G, P5)
                mark(CP(cU[0:64], cc[0:64]), "prep_in")
                mark(TSC(cU[64:128], cc[64:128], -1.0, None, ALU.mult), "prep_in")
                mark(TSC(cV[0:64], cc[64:128], -1.0, None, ALU.mult), "prep_in")
                mark(TSC(cV[64:128], cc[0:64], -1.0, None, ALU.mult), "prep_in")
                e.wait_ge(S("x0_mm"), 1)
                mark(CP(x0, bank(6, NB, G)), "prep_in")
                mark(CP(x0s, bank(6, NB, G, at=256)), "prep_in")

            e.sem_inc(w_lo, 2)
            e.sem_inc(mm_done, 2)
            e.sem_inc(ps_free, 2)
            conv(0, 0, 0)
            e.wait_ge(s_load, 7 * 16)
            for k in range(KD):
                e.wait_ge(S("x_tr"), k + 1)
                mark(CP(h[:, k, :], bank(4 + 2 * (k % 2), T)), "x_ev")
                e.wait_ge(x_hi, k + 1)
                STT(xl[:, k, :], h[:, k, :], gains[:, G_FFN1, k:k + 1], xh[:, k, :].bitcast(F32), ALU.mult, ALU.subtract).then_inc(x_lo, 1)
            rms(0)
            ffn(0)
            for r in range(8):
                e.wait_ge(S("kt_mm"), r + 1)
                mark(CP(Kt[:, 4 * r:4 * r + 4, :], bank(6 + r % 2, 4, P, rows=P5)), "kt_ok")
            rms(1)
            own(TTT(ktmp, ident[0:P5, None, 0:P5].broadcast_to([P5, G, P5]), dd[:, :, None].broadcast_to([P5, G, P5]), ALU.mult))
            mark(TTT(Kt[:, :, 0:P5], Kt[:, :, 0:P5], ktmp, ALU.add), "ktd_ok")
            e.wait_ge(S("wzg_in"), 16)
            e.wait_ge(s_load, 7 * 16)
            mark(TTT(wzg, wzg, gains[:, G_MIX, :][:, :, None].broadcast_to([P, KD, RANK]), ALU.mult), "wzg_ok")

            def proj(f0, scales):
                def body(i, n, par):
                    f = i * 2 + (f0 + par)
                    TTT(two(chunk(PR, f)), halves(2 * par), two(R[:]), ALU.mult).then_inc(ps_free, 1)
                return body

            group(W_IN, proj(0, True))
            e.wait_ge(S("tt_in"), 16 * L5)
            group(W_IN + 1, proj(8, False))
            e.wait_ge(S("zg_mm"), 1)
            mark(TTT(two(zg[0:RANK, :]), PS[0:RANK, 6:8, 0:TH], two(R[0:RANK, :]), ALU.mult), "zg_ok")
            e.wait_ge(S("tables_ok"), 1)

            def one_col(t, j):
                return t[:, :, j:j + 1].rearrange("p g a -> p (g a)")

            for r in range(5):
                n = min(G, 7 * r + 7) - 7 * r
                e.wait_ge(S("u2_mm"), r + 1)
                mark(CP(u2[:, 7 * r:7 * r + n, :], bank(2 + r % 2, n, C5)), "u2_ok")
            for r in range(5):
                n = min(G, 7 * r + 7) - 7 * r
                gg = slice(7 * r, 7 * r + n)
                e.wait_ge(S("d_mm"), r + 1)
                d, dw = bank(4 + 2 * (r % 2), n, C5), bank(5 + 2 * (r % 2), n, C5)
                tw = view(SG, 0, n, C5P)
                own(TTT(zin[:, gg, :], d[:, :, 0:C5P], tc[:, gg, :], ALU.mult))
                own(TTT(tw, dw[:, :, 0:C5P], sg[:, gg, :], ALU.mult))
                own(TTT(zin[:, gg, :], zin[:, gg, :], tw, ALU.add))
                mark(TTT(s1[:, :, gg].rearrange("p b g -> p g b"), d[:, :, C5P:C5], s1[:, :, gg].rearrange("p b g -> p g b"), ALU.add), "d_ok")
            own(TTT(keep5, sm[:, 4, :][:, :, None].broadcast_to([P, G, C5P]), chunk_keep[:, None, :].broadcast_to([P, G, C5P]), ALU.mult))
            fl = "p g c -> p (g c)"
            own(e.tensor_tensor_scan(zz.rearrange(fl), keep5.rearrange(fl), zin.rearrange(fl), 0.0, ALU.mult, ALU.add))
            own(CP(zin[0:64], zz[64:128]))
            own(CP(zin[64:128], zz[0:64]))
            own(TTT(zin, zin, sg, ALU.mult))
            own(TTT(zz, zz, tc, ALU.mult))
            own(e.memset(XS[:, :, 0:1], 0.0))
            own(TTT(XS[:, :, 1:C5P], zz[:, :, 0:C5P - 1], zin[:, :, 0:C5P - 1], ALU.subtract))
            own(TTT(sm[:, 14, :], one_col(zz, C5P - 1), one_col(zin, C5P - 1), ALU.subtract))
            e.sem_inc(S("s1_ok"), 1)
            mark(CP(XS[:, :, C5P:C5], x0.rearrange("p b g -> p g b")), "xs_ok")
            e.wait_ge(S("s1_mm"), 1)
            own(CP(s1o[:, 0:2, :], bank(2, 2, P)))
            mark(CP(s1o[0:G, 2, :], bank(2, P, at=2 * P, rows=G)), "s1o_ok")
            for j in range(L5):
                e.wait_ge(S("zt_mm"), j + 1)
                mark(CP(zT[:, :, j::L5], bank(4 + j % 2, 4, C5)), "zt_ok")
            for f in range(4):
                e.wait_ge(S("sig_ok"), f + 1)
                mark(TTT(og, zT[:, f, :], sig, ALU.mult), "so_ok")
                e.wait_ge(S("mix_hi"), 1 + f)
                mark(TTT(yl[:, 4 + f, :], og, yh[:, 4 + f, :].bitcast(F32), ALU.subtract), "mix_ok")
            q, k_ = PR[:, 0:2, :], PR[:, 2:4, :]
            own(TSC(q, q, DK ** -0.5, None, ALU.mult))
            e.wait_ge(S("z_mm"), 1)
            e.wait_ge(S("d_gla"), 16 * 3)
            for i in range(2):
                mark(TSC(two(zb[:, i, :]), halves(2 * i), bgate[:, i:i + 1], None, ALU.add), "z_sb")
            e.wait_ge(S("ln_ok"), 1)
            own(STT(ge, zb, 0.0, zt, ALU.min, ALU.subtract))
            for i in range(2):
                own(e.tensor_tensor_scan(zb[:, i, :], scan_keep, ge[:, i, :], 0.0, ALU.mult, ALU.add))

            def against(dst, t0, t1, size, at):
                n = (t1 - t0) // size
                bb = zb[:, :, t0:t1].rearrange("p a (n s) -> p a n s", s=size)
                return TTT(dst[:, :, t0:t1].rearrange("p a (n s) -> p a n s", s=size),
                           bb[:, :, :, at:at + 1].broadcast_to([P, 2, n, size]), bb, ALU.subtract)

            mark(against(ge, 0, TP, CH, CH - 1), "ke_rel")
            mark(against(ge, TP, T, BT, BT - 1), "ke_rel")
            e.wait_ge(S("ke_exp"), 1)
            mark(TTT(gk, k_, ge, ALU.mult), "ke_ok")
            e.wait_ge(S("sc_zero"), 5)

            def take(r):
                e.wait_ge(S("lev_mm"), r + 1)
                own(e.copy_predicated(SCp, level_mask[:, r, :][:, None, None, :].broadcast_to([P, H, 4, CH]),
                                      PS[:, 0:4, 0:256].rearrange("p h (j t) -> p h j t", j=4)))
                if r <= 3:
                    own(e.copy_predicated(SCs[0:TS], level_mask[0:TS, r, :][:, None, :].broadcast_to([TS, H, CH]),
                                          PS[0:TS, 0:4, 256:320]))
                e.sem_inc(S("lev_ok"), 1)

            for lv, hs in enumerate(LEVELS):
                TL = T if hs <= 4 else TP
                mark(against(ge, 0, TL, 2 * hs, hs - 1), "rel_ok")
                take(lv)
                e.wait_ge(S("ktok_mm"), NT)
                e.wait_ge(S("e_ok"), lv + 1)
                own(TTT(gq[:, :, 0:TL], q[:, :, 0:TL], ge[:, :, 0:TL], ALU.mult))
                mark(TTT(gk[:, :, 0:TL], k_[:, :, 0:TL], ge[:, :, 0:TL], ALU.mult), "lev_in")
            take(len(LEVELS))
            for a in range(2):
                own(CP(SC[a * CH:(a + 1) * CH, :, 0:4, a * CH:(a + 1) * CH], SCp[a * CH:(a + 1) * CH]))
            mark(CP(SC[0:TS, :, 4, 0:CH], SCs[0:TS]), "sc_ok")
            e.wait_ge(S("eb_ok"), 1)
            mark(TTT(gq, q, ge, ALU.mult), "qe_ok")
            e.wait_ge(S("ktok_ok"), NT)
            e.wait_ge(S("vtok_ok"), NT)
            for b in range(NB):
                own(TSC(kem[:, b, :], ktok[0:TS, 4, :], batch_rows[0:TS, b:b + 1], None, ALU.mult))
            e.sem_inc(S("kem_ok"), 1)
            e.wait_ge(S("kv_mm"), 1)
            for c in range(NCH):
                for f in range(2):
                    own(STT(Sall[:, f, c + 1, :], Sall[:, f, c, :], ge[:, f, c * CH + CH - 1:c * CH + CH],
                            PS[:, 4 + 2 * f + c % 2, (c // 2) * DV:(c // 2 + 1) * DV], ALU.mult, ALU.add))
            e.sem_inc(S("st_ok"), 1)
            e.wait_ge(S("s0_in"), 32)
            e.wait_ge(S("kvs_mm"), 1)
            for b in range(NB):
                for f in range(2):
                    t1 = TP + b * BT + BT - 1
                    if b == 0 and f == 0:
                        e.wait_ge(s5_out, 16 * 6)
                    own(STT(Snew[:, f, b, :], S0[:, f, b, :], ge[:, f, t1:t1 + 1],
                            PS[:, 2 * f + b // 4, (b % 4) * DV:(b % 4 + 1) * DV], ALU.mult, ALU.add))
            e.sem_inc(S("sts_ok"), 1)
            e.sem_inc(S("snew_ok"), 1)
            for hd in range(H):
                e.wait_ge(S("o_mm"), hd + 1)
                mark(CP(oT[:, hd, :], bank(4 * (hd // 2) + 2 * (hd % 2), T)), "o_sb")
            mark(e.memset(bank(0, 20), 1.0), "oss_zero")
            e.wait_ge(S("ort"), 1)
            own(TSC(rv[:, 1, :], bank(0, 20), 1.0 / DV, EPS, ALU.mult, ALU.add))
            inverse(20, DV)
            for hd in range(H):
                for j in range(NT):
                    n = hd * NT + j
                    if n >= 2:
                        e.wait_ge(S("orb"), n - 1)
                    TSC(diag[:, n % 2, :], ident, rv[:, 3, n:n + 1], None, ALU.mult).then_inc(S("odg"), 1)
                e.wait_ge(S("orb"), (hd + 1) * NT)
                if hd:
                    e.wait_ge(S("mix_hi"), 4 + hd)
                mark(STT(us[:], oT[:, hd, :], ggla[:, 0:1], bank(2 + 2 * (hd % 2), T), ALU.mult, ALU.mult), "orr_ok")
                e.wait_ge(S("rs_ok"), hd + 1)
                mark(TTT(us[:], us[:], act[:], ALU.mult), "og_ok")
                e.wait_ge(S("mix_hi"), 4 + hd + 1)
                mark(TTT(yl[:, hd, :], us[:], yh[:, hd, :].bitcast(F32), ALU.subtract), "mix_ok")
            group(W_OUT, down(groups[W_OUT]))
            e.wait_ge(S("mrt"), 1)
            own(TSC(rv[:, 1, 0:2], mst[:, 0:2], 1.0 / D, EPS, ALU.mult, ALU.add))
            own(CP(rv[:, 0, 0:2], mst[:, 2:4]))
            inverse(2, D)
            for j in range(2):
                mark(TSC(mnat[:, j, :], mnat[:, j, :], rv[:, 3, j:j + 1], None, ALU.mult), "mem_ok")
            for k in range(KD):
                e.wait_ge(S("memx_hi"), k + 1)
                STT(ml[:, k, :], bank(4 + k % 2, M), gains[:, G_MEM, k:k + 1], mh[:, k, :].bitcast(F32),
                    ALU.mult, ALU.subtract).then_inc(S("memx_lo"), 1)

            def kv(i, n, par):
                CP(chunk(KVT, i * 2 + par), bank(2 * par, M)).then_inc(ps_free, 1)

            group(KV, kv)
            for r in range(8):
                e.wait_ge(S("nat_mm"), r + 1)
                mark(CP(KVN[:, r // 4, (r % 4) * 512:(r % 4 + 1) * 512], bank(4 + r % 2, 512)), "nat_ok")
            rms(2)
            group(W_Q, proj(0, False))

            def softmax(r, w):
                e.wait_ge(S("s_mm"), r + 1)
                own(e.tensor_reduce(att[0:w, 0:4], bank(4, H, M, rows=w), AX, ALU.max))
                mark(TSC(att[0:w, 4:8], att[0:w, 0:4], -(CD ** -0.5), None, ALU.mult), "mx_ok")
                e.wait_ge(S("exp_ok"), H * (r + 1))
                own(e.reciprocal(att[0:w, 12:16], att[0:w, 8:12]))
                for hd in range(H):
                    own(TSC(pp[0:w, hd, :], pp[0:w, hd, :], att[0:w, 12 + hd:13 + hd], None, ALU.mult))
                e.sem_inc(S("p_ok"), 1)
                e.wait_ge(S("pt_mm"), r + 1)

            for r in range(4):
                softmax(r, P)
                mark(CP(PT[:, :, :, r * P:(r + 1) * P].rearrange("p h j t -> p (h j) t"), bank(6, 8, P)), "pt_ok")
            for f in range(8):
                e.wait_ge(S("pv_hi"), f + 1)
                mark(TTT(yl[:, f, 0:TP], bank(4 + f % 2, TP), yh[:, f, 0:TP].bitcast(F32), ALU.subtract), "pv_lo")

            def decode_max(c):
                e.wait_ge(S("ssm_mm"), 8 * (c + 1))
                own(e.tensor_reduce(att[:, c:c + 1], bank(6 + c, M), AX, ALU.max))
                mark(TSC(att[:, 4 + c:5 + c], att[:, c:c + 1], -(CD ** -0.5), None, ALU.mult), "mx_ok")

            def decode_probs(c):
                e.wait_ge(S("exp_ok"), 4 * H + c + 1)
                own(e.reciprocal(att[:, 12 + c:13 + c], att[:, 8 + c:9 + c]))
                mark(TSC(pp[:, c, :], pp[:, c, :], att[:, 12 + c:13 + c], None, ALU.mult), "p_ok")

            def decode_turned(c):
                e.wait_ge(S("pt_mm"), 5 + c)
                e.wait_ge(S("ptz_zero"), 1)
                for q in range(4):
                    own(CP(PTz[:, :, :, 4 * c + q, BT * q:BT * q + BT], bank(4 + c, 2, H, 4, BT)[:, :, :, q, :]))
                e.sem_inc(S("pt_ok"), 1)

            for b in range(NB):
                e.wait_ge(S("kbt_mm"), 2 * b + 2)
                if b:
                    e.wait_ge(S("ssm_mm"), 2 * b)
                mark(CP(KBT[:, 4:8, :].rearrange("p f m -> p (f m)"), bank(2, 1024)), "kbt_v")
                if b == 4:
                    decode_max(0)
                if b == 6:
                    decode_probs(0)
            decode_turned(0)
            decode_max(1)
            decode_probs(1)
            decode_turned(1)
            for c in range(2):
                e.wait_ge(S("pvs_mm"), 4 * (c + 1))
                mark(CP(os[:, c, :], bank(c, M)), "os_ok")
            for c in range(2):
                e.wait_ge(S("pvs_hi"), c + 1)
                tt = slice(TP + 32 * c, TP + 32 * c + 32)
                mark(TTT(yl[:, :, tt].rearrange("p (h f) t -> p f h t", f=2), bank(2 + c, 2, H, 32),
                         yh[:, :, tt].bitcast(F32).rearrange("p (h f) t -> p f h t", f=2), ALU.subtract), "pvs_lo")
            group(W_O, down(groups[W_O]))
            rms(3)
            ffn(FFN2)
            rms(4)
            for k in range(KD):
                mark(STT(yy[:, k, :], h[:, k, :], gains[:, G_FINAL, k:k + 1], R[:], ALU.mult, ALU.mult), "yy_ok")
            for j in range(NT):
                w = min(P, T - j * P)
                e.wait_ge(S("y_tr"), j + 1)
                if j >= 2:
                    e.wait_ge(y_out[j % 2], 16 * (j // 2))
                mark(CP(yo[0:w, j % 2, :], bank(2 * (j % 2), D, rows=w)), "yo_ok")


_INS = ["x_prompt", "x_sample", "state_gla", "state_s5_re", "state_s5_im", "cache_mem_k", "cache_mem_v", "mem_prompt",
        "g_ffn1", "w_ffn1_gu", "w_ffn1_down", "g_mix", "w_in", "w_gla_gate", "b_gla_gate", "g_gla_out", "s5_lambda_re",
        "s5_lambda_im", "s5_log_dt", "s5_b_re", "s5_b_im", "s5_c_re", "s5_c_im", "s5_d", "s5_w_glu", "s5_b_glu", "w_out",
        "g_cross", "g_mem", "w_cq", "w_ckv", "w_co", "g_ffn2", "w_ffn2_gu", "w_ffn2_down", "g_final"]
_OUTS = [("y_p", (1, TP, D)), ("y_s", (NB, BT, D)), ("gla_p", (1, 1, H, DK, DV)), ("s5_re_p", (1, 1, G, N5)),
         ("s5_im_p", (1, 1, G, N5)), ("mem_k", (1, 1, M, H, CD)), ("mem_v", (1, 1, M, H, CD)),
         ("gla_s", (1, NB, H, DK, DV)), ("s5_re_s", (1, NB, G, N5)), ("s5_im_s", (1, NB, G, N5))]


def constants():
    import numpy as np
    c = np.zeros((P, C_END), np.float32)
    c[:, C_ID:C_ID + P] = np.eye(P)
    t = np.arange(T)
    c[:, C_SCAN:C_SCAN + T] = np.where(t < TP, t % CH, t % BT) != 0
    s, u = np.arange(P)[:, None] % CH, np.arange(CH)[None, :]
    levels = [s == u] + [(s // (2 * n) == u // (2 * n)) & (s % (2 * n) < n) & (u % (2 * n) >= n) for n in LEVELS]
    c[:, C_MASK:C_MASK + 7 * CH] = np.concatenate(levels, axis=1)
    c[:, C_CHUNK:C_CHUNK + C5P] = np.arange(C5P) != 0
    c[:, C_BATCH:C_BATCH + NB] = np.arange(P)[:, None] // BT == np.arange(NB)[None, :]
    return c


def kernel(**inputs):
    import numpy as _np
    import concourse.bacc as _bacc
    from concourse import mybir as _mybir
    from concourse.bass_utils import run_bass_kernel_spmd as _run

    nc = _bacc.Bacc("TRN2", target_bir_lowering=False, num_devices=1, dynamic_dma_scratch_size=1024)
    arrays, A, O = {}, {}, {}
    for name in _INS:
        a = _np.ascontiguousarray(inputs[name])
        arrays[f"in_{name}"] = a
        A[name] = nc.dram_tensor(f"in_{name}", a.shape, _mybir.dt.from_np(a.dtype), kind="ExternalInput").ap()
    c = constants()
    arrays["in_constants"] = c
    consts = nc.dram_tensor("in_constants", c.shape, _mybir.dt.float32, kind="ExternalInput").ap()
    for name, shape in _OUTS:
        O[name] = nc.dram_tensor(f"out_{name}", shape, _mybir.dt.float32, kind="ExternalOutput").ap()
    hymba_kernel(nc, A, O, consts)
    r = _run(nc, [arrays], core_ids=[0])
    return tuple(r.results[0][f"out_{name}"] for name, _ in _OUTS)
```

```python
import math
from contextlib import ExitStack

import concourse.bass as bass
from concourse import mybir

F32 = mybir.dt.float32
F32R = mybir.dt.float32r
I32 = mybir.dt.int32
ALU = mybir.AluOpType
ACT = mybir.ActivationFunctionType
AX = mybir.AxisListType.X

P = 128
D = 1024
KD = D // P
TP, NB, BT = 512, 8, 8
TS = NB * BT
T = TP + TS
TH = T // 2
NT = (T + P - 1) // P
F = 2816
FT = F // P
FGROUPS = (8, 8, 6)
EPS = 1e-6
H, DK, DV, RANK = 4, 64, 128, 16
TAU = 16.0
CH = 64
LEVELS = (1, 2, 4, 8, 16, 32)
NCH = TP // CH
G, N5, P5 = 32, 64, 16
L5 = 8
C5P = TP // L5
C5 = T // L5
M = 256
CD = 256
TWO_PI = 6.283185307179586
PI_A, PI_B = 6.28125, 0.0019350051879882812
PI_C = TWO_PI - PI_A - PI_B
LN2_HI, LN2_LO = 0.693359375, -2.12194440054690581e-4
ROUND = 12582912.0

MW = 10752
C_ID, C_SCAN, C_MASK, C_CHUNK, C_BATCH = 0, P, P + T, P + T + 7 * CH, P + T + 7 * CH + C5P
C_END = C_BATCH + NB
G_FFN1, G_MIX, G_CROSS, G_FFN2, G_FINAL, G_MEM = range(6)


def hymba_kernel(nc, A, O, consts):
    with ExitStack() as ctx:
        def sb(name, shape, dt=F32):
            return ctx.enter_context(nc.sbuf_tensor(name, shape, dt))

        def alias(name, floats):
            with nc.sbuf_tensor(name, [P, floats], F32) as t:
                return t

        sems = {}

        def S(name):
            if name not in sems:
                sems[name] = ctx.enter_context(nc.semaphore(name))
            return sems[name]

        cst = sb("cst", [P, C_END])
        ident = cst[:, C_ID:C_ID + P]
        scan_keep = cst[:, C_SCAN:C_SCAN + T]
        level_mask = cst[:, C_MASK:C_MASK + 7 * CH].bitcast(I32).rearrange("p (l t) -> p l t", l=7)
        chunk_keep = cst[:, C_CHUNK:C_CHUNK + C5P]
        batch_rows = cst[:, C_BATCH:C_BATCH + NB]
        mean_d, mean_dv = sb("mean_d", [P, P]), sb("mean_dv", [P, P])
        gains = sb("gains", [P, 6, KD])
        eps = sb("eps", [P, 1])
        one = sb("one", [P, 1])
        h = sb("h", [P, KD, T])
        Xs = alias("Xs", 2 * KD * T)
        xh = sb("xh", [P, KD, T], F32R)
        xl = sb("xl", [P, KD, T], F32R)
        Hs = alias("Hs", 2 * KD * T)
        yh = sb("yh", [P, KD, T], F32R)
        yl = sb("yl", [P, KD, T], F32R)
        raw = sb("raw", [P, 2, KD * P])
        wh = sb("wh", [P, 2, KD * P], F32R)
        wl = sb("wl", [P, 2, KD * P], F32R)
        acc = sb("acc", [P, NT * P])
        sq = sb("sq", [P, 2, T])
        R = sb("R", [P, T])
        gua = sb("gua", [P, 3, T])
        gs, us, act = (gua[:, i, :] for i in range(3))
        mst = sb("mst", [P, 6])
        AR = sb("AR", [P, 16 * T + MW])
        PR = AR[:, 0:16 * T].rearrange("p (f t) -> p f t", t=T)
        MM = AR[:, 16 * T:16 * T + MW]

        def view(base, at, *dims):
            n = 1
            for d in dims:
                n *= d
            v = base[:, at:at + n]
            if len(dims) == 1:
                return v
            names = "abcd"[:len(dims)]
            return v.rearrange(f"p ({' '.join(names)}) -> p {' '.join(names)}",
                               **{k: d for k, d in zip(names[1:], dims[1:])})

        PS = ctx.enter_context(nc.psum_tensor("PS", [P, 8, 512], F32))

        def bank(b, *dims, at=0, rows=P):
            n = 1
            for d in dims:
                n *= d
            v = PS[0:rows, :, :].rearrange("p b n -> p (b n)")[:, b * 512 + at:b * 512 + at + n]
            if len(dims) == 1:
                return v
            names = "abcd"[:len(dims)]
            return v.rearrange(f"p ({' '.join(names)}) -> p {' '.join(names)}",
                               **{k: d for k, d in zip(names[1:], dims[1:])})

        zb = gua[:, 1:3, :]
        ge = (view(MM, 1152, 2, T), view(Hs, 4608, 2, T))
        gq = (view(MM, 2304, 2, T), view(Hs, 0, 2, T))
        gk = (view(MM, 3456, 2, T), view(Hs, 1152, 2, T))
        vtok = view(MM, 4608, NT, H * DV)
        zg = gs[:]
        zt = sq[:]
        wgate = view(MM, 8896, H * DK)
        bgate = view(MM, 9152, 2)
        ggla = view(MM, 9154, 1)
        wzg = view(MM, 9168, KD, RANK)
        Sall = view(Xs, 0, 2, NCH + 1, DV)
        S0 = view(Xs, 2304, 2, NB, DV)
        SC = view(Xs, 4352, H, NT, P)
        ktok = view(Xs, 6912, NT, 2 * P)
        kem = AR[0:TS, 4 * T:4 * T + NB * 2 * P].rearrange("p (b k) -> p b k", b=NB)
        oT = PR[:, 4:8, :]
        CA = view(MM, 0, G, L5 + 1, P5)
        tc = view(MM, 4608, G, C5P)
        sg = view(MM, 6656, G, C5P)
        sm = view(MM, 9296, 15, G)
        x0 = view(MM, 9776, NB, G)
        s1 = view(MM, 10032, NB, G)
        bglu = view(MM, 10288, 4)
        Win = view(Hs, 0, G, P)
        TT = view(Hs, 4096, G, P)
        bU, bV, BV, Bb = (view(AR, 512 * i, G, P5) for i in range(4))
        cU, cV = (view(AR, 2048 + 512 * i, G, P5) for i in range(2))
        pr, pi = (view(AR, 3072 + 288 * i, G, L5 + 1) for i in range(2))
        prr, pir = (view(AR, 3648 + 256 * i, G, L5) for i in range(2))
        x0s = view(AR, 4160, NB, G)
        dd = AR[0:P5, 4416:4416 + G]
        prep = AR[:, 4448:5120]
        WT = view(AR, 5120, G, L5, P5)
        Kt = AR[0:P5, 5120:9216].rearrange("p (g j) -> p g j", g=G)
        ktmp = AR[0:P5, 0:G * P5].rearrange("p (g q) -> p g q", g=G)
        nat = view(MM, 5120, 4, P)
        nat2 = view(MM, 5632, 4, P)
        x0n = view(MM, 6144, 2, P)
        x0sn = view(MM, 6400, 2, P)
        u2 = view(Xs, 0, G, C5)
        SF = Xs[:, 2304:6400]
        UT = SF[0:C5, :].rearrange("p (g s q) -> p g s q", g=G, s=L5)
        zin = view(SF, 0, G, C5P)
        zz = view(SF, 2048, G, C5P)
        Y2 = SF[0:C5, :].rearrange("p (t j) -> p t j", t=L5)
        SG = Xs[:, 6400:8704]
        XS = view(SG, 0, G, C5)
        keep5 = view(SG, 0, G, C5P)
        wglu = view(Xs, 8704, 4, P)
        zin_tmp = SF[:, 2048:4096]
        zT = view(SG, 0, 4, T)
        sig = view(Xs, 0, T)
        og = view(Xs, 576, T)
        s1o = view(AR, 12 * T, 3, P)
        Snew = view(AR, 12 * T, 2, NB, DV)
        SCp = view(MM, 9600, H, 4, CH)
        SCs = view(Xs, 8192, H, CH)
        oroot = (sq[:, 0, :], sq[:, 1, :])
        osq = (gs, ge[0][:, 0, :], gk[0][:, 0, :], gq[0][:, 0, :])
        KVT = view(MM, 0, 16, M)
        KVN = view(MM, 4096, 2, 2 * D)
        mh = yh[:, :, 0:M]
        ml = yl[:, :, 0:M]
        mnat = view(MM, 4096, 2, D)
        msq = view(MM, 6144, D)
        qT = PR[:, 0:8, :]
        PT = view(AR, 8 * T, H, 2, TP)
        KB = [view(Xs, 4096, 2, D), view(Xs, 6144, 2, D), view(MM, 0, 2, D), view(MM, 2048, 2, D)]
        KBT = view(MM, 8192, KD, M)
        pp = view(Xs, 0, H, M)
        att = view(Xs, 1024, 16)
        os = view(Xs, 1040, 2, M)
        qz = view(Xs, 2048, KD, NB, 4 * BT)
        PTz = view(MM, 4096, 2, H, NB, 4 * BT)
        yy = PR[:, 0:8, :]
        yo = view(MM, 0, 2, D)
        xin = view(MM, 0, NT, D)

        groups = []

        def add(kind, src, nblk, K, row0, cols, **kw):
            n0 = sum(g["n"] for g in groups)
            groups.append(dict(kind=kind, src=src, n=nblk, K=K, row0=row0, cols=cols, n0=n0, **kw))

        def ffn(which):
            f0 = 0
            for i, nf in enumerate(FGROUPS):
                add("gu", A[f"w_ffn{which}_gu"], 2 * nf, KD, 0, (f0 * P, F + f0 * P, P), f0=f0 + (which - 1) * FT)
                add("down", A[f"w_ffn{which}_down"], KD, nf, f0 * P, (0, P, 2 * P),
                    norm=(1 if which == 1 else 4) if i == 2 else None, half=True)
                f0 += nf

        ffn(1)
        add("proj", A["w_in"], 8, KD, 0, (0, P, 2 * P), f0=0, first=True)
        add("proj", A["w_in"], 8, KD, 0, (D + RANK, D + RANK + P, 2 * P), f0=8)
        add("down", A["w_out"], KD, KD, 0, (0, P, 2 * P), norm=2, half=False)
        add("kv", A["w_ckv"], 16, KD, 0, (0, P, 2 * P))
        add("q", A["w_cq"], KD, KD, 0, (0, P, 2 * P))
        add("down", A["w_co"], KD, KD, 0, (0, P, 2 * P), norm=3, half=False)
        ffn(2)
        W_IN, W_OUT, KV, W_Q, W_O, FFN2 = 6, 8, 9, 10, 11, 12
        gain_of = {0: G_FFN1, 1: G_MIX, 2: G_CROSS, 3: G_FFN2, 4: G_FINAL}

        s_load, s_const = S("s_load"), S("s_const")
        s_x, x_ev = S("s_x"), S("x_ev")
        raw_in = [S("raw_in0"), S("raw_in1")]
        w_hi = S("w_hi")
        w_lo = S("w_lo")
        mm_done = S("mm_done")
        ps_free = S("ps_free")
        sq_ready, acc_ready = S("sq_ready"), S("acc_ready")
        x_hi, x_lo = S("x_hi"), S("x_lo")
        acc_zero = S("acc_zero")
        ss, rt, r_ready = S("ss"), S("rt"), S("r_ready")
        g_scaled, g_act, u_scaled, hid, hid_hi, hid_lo = (S(n) for n in (
            "g_scaled", "g_act", "u_scaled", "hid", "hid_hi", "hid_lo"))
        gla_out, s5_out, kv_out = S("gla_out"), S("s5_out"), S("kv_out")
        y_out = [S("y_out0"), S("y_out1")]

        block = ctx.enter_context(nc.Block())

        class Mark:

            def __init__(self, eng):
                self.eng, self.n = eng, {}

            def __call__(self, ins, name, by=1):
                ins.then_inc(S(name), by)
                self.n[name] = self.n.get(name, 0) + by
                self.eng.wait_ge(S(name), self.n[name])

        def chunk(t, k):
            return t[:, bass.ds(k, 1), :].rearrange("p a t -> p (a t)")

        @block.sync
        def _(e):
            e.dma_start(cst[:], consts).then_inc(s_load, 16)
            with nc.allow_non_contiguous_dma(reason="gains, 4 KB each"):
                for i, name in enumerate(("g_ffn1", "g_mix", "g_cross", "g_ffn2", "g_final", "g_mem")):
                    g = A[name] if name == "g_final" else A[name][0]
                    e.dma_start(gains[:, i, :], g.rearrange("(k p) -> p k", p=P)).then_inc(s_load, 16)
            e.dma_start(xin[:, 0:4, :], A["x_prompt"][0].rearrange("(n p) d -> p n d", p=P)).then_inc(s_x, 16)
            e.dma_start(xin[0:TS, 4, :], A["x_sample"].rearrange("b t d -> (b t) d")).then_inc(s_x, 16)
            for g in groups:
                K, (c0, c1, step) = g["K"], g["cols"]
                src = g["src"][0, g["row0"]:g["row0"] + K * P, :].rearrange("(k p) n -> p k n", p=P)

                def load(i):
                    for par in range(2):
                        e.wait_ge(w_lo, i * 2 + (g["n0"] + par + 1))
                        e.dma_start(raw[:, par, 0:K * P].rearrange("p (k n) -> p k n", k=K),
                                    src[:, :, bass.ds(i * step + (c0, c1)[par], P)]).then_inc(raw_in[par], 16)

                first = 0
                if g is groups[W_O]:
                    first = 1
                    load(0)
                    for n in range(2 * NB):
                        if n < 2:
                            e.wait_ge(mm_done, groups[W_O]["n0"] + 2)
                        elif n < 4:
                            e.wait_ge(S("s_mm"), 4)
                        elif n < 4 + NB:
                            e.wait_ge(S("kbt_mm"), 2 * (n - 4) + 2)
                        else:
                            e.wait_ge(S("pvs_mm"), n - 4 - NB + 1)
                        kv_src = A["cache_mem_k" if n < NB else "cache_mem_v"][0, n % NB]
                        e.dma_start(KB[n % 4], kv_src.rearrange("(j p) h d -> p j (h d)", p=P)).then_inc(S(f"kb_in{n % 4}"), 16)
                with e.Fori(first, g["n"] // 2) as i:
                    load(i)

        @block.gpsimd
        def _(e):
            e.memset(mean_d[:], 1.0 / D).then_inc(s_const, 1)
            e.memset(mean_dv[:], 1.0 / DV).then_inc(s_const, 1)
            e.memset(eps[:], EPS).then_inc(s_const, 1)
            e.memset(one[:], 1.0).then_inc(s_const, 1)
            e.memset(acc[:, T:], 0.0).then_inc(s_const, 1)

            def sums(m):
                if m:
                    e.wait_ge(ss, m)
                    e.wait_ge(acc_ready, 8 * m)
                e.memset(acc[:, 0:T], 0.0).then_inc(acc_zero, 1)
                e.wait_ge(acc_zero, m + 1)
                for k in range(KD):
                    e.wait_ge(sq_ready, 8 * m + k + 1)
                    if 8 * m + k:
                        e.wait_ge(acc_ready, 8 * m + k)
                    e.tensor_tensor(acc[:, 0:T], acc[:, 0:T], sq[:, k % 2, :], ALU.add).then_inc(acc_ready, 1)

            mark = Mark(e)
            TTT, TSC = e.tensor_tensor, e.tensor_scalar

            def own(ins):
                mark(ins, "pool_own")

            def mul(o, a, b):
                own(TTT(o, a, b, ALU.mult))

            def poly(o, x, coeffs):
                own(TSC(o, x, coeffs[0], coeffs[1], ALU.mult, ALU.add))
                for c in coeffs[2:]:
                    mul(o, o, x)
                    own(TSC(o, o, c, None, ALU.add))

            def exp(o, x, k, pw):
                own(TSC(x, x, 88.0, -87.0, ALU.min, ALU.max))
                own(TSC(k, x, 1.4426950408889634, ROUND, ALU.mult, ALU.add))
                own(TSC(k, k, -ROUND, None, ALU.add))
                for part in (LN2_HI, LN2_LO):
                    own(TSC(pw, k, -part, None, ALU.mult))
                    own(TTT(x, x, pw, ALU.add))
                poly(o, x, [1.0 / math.factorial(i) for i in range(8, -1, -1)])
                own(TSC(k, k, 127.0, 8388608.0, ALU.add, ALU.mult))
                own(e.tensor_copy(pw.bitcast(I32), k))
                mul(o, o, pw)

            def times(o_r, o_i, a_r, a_i, b_r, b_i, u, v):
                mul(u, a_r, b_r)
                mul(v, a_i, b_i)
                own(TTT(o_r, u, v, ALU.subtract))
                mul(u, a_r, b_i)
                mul(v, a_i, b_r)
                own(TTT(o_i, u, v, ALU.add))

            def one_col(t, j):
                return t[:, :, j:j + 1].rearrange("p g a -> p (g a)")

            def wide(t, n):
                return t[:, :, None].broadcast_to([P, G, n])

            def s5_parameters():
                dt, dr, th, mag, r8, sn, cs, lr, li, t0, t1, t2, fr, fi = (sm[:, i, :] for i in range(14))
                e.wait_ge(S("prep_in"), 8)
                e.wait_ge(S("d_s5"), 16 * 12)
                exp(t0, dt, t1, t2)
                own(e.tensor_copy(dt, t0))
                mul(dr, dt, lr)
                mul(th, dt, li)
                own(TSC(t1, th, 1.0 / TWO_PI, None, ALU.mult))
                own(TSC(t1, t1, ROUND, None, ALU.add))
                own(TSC(t1, t1, -ROUND, None, ALU.add))
                for part in (PI_A, PI_B, PI_C):
                    own(TSC(t0, t1, -part, None, ALU.mult))
                    own(TTT(th, th, t0, ALU.add))
                own(TSC(th, th, 0.5, None, ALU.mult))
                exp(mag, dr, t1, t2)
                mul(r8, mag, mag)
                mul(r8, r8, r8)
                mul(r8, r8, r8)
                mul(t0, th, th)
                poly(t1, t0, [(-1.0) ** i / math.factorial(2 * i + 1) for i in range(7, -1, -1)])
                mul(t1, t1, th)
                poly(t2, t0, [(-1.0) ** i / math.factorial(2 * i) for i in range(8, -1, -1)])
                mul(sn, t1, t2)
                own(TSC(sn, sn, 2.0, None, ALU.mult))
                mul(cs, t1, t1)
                own(TSC(cs, cs, -2.0, 1.0, ALU.mult, ALU.add))
                own(e.memset(pr[:, :, 0:1], 1.0))
                own(e.memset(pi[:, :, 0:1], 0.0))
                ar, ai = one_col(pr, 1), one_col(pi, 1)
                mul(ar, mag, cs)
                mul(ai, mag, sn)
                own(TSC(t1, ar, -1.0, None, ALU.add))
                mul(fr, t1, lr)
                mul(t2, ai, li)
                own(TTT(fr, fr, t2, ALU.add))
                mul(fr, fr, sm[:, 14, :])
                mul(fi, ai, lr)
                mul(t2, t1, li)
                own(TTT(fi, fi, t2, ALU.subtract))
                mul(fi, fi, sm[:, 14, :])
                for w in (1, 2, 4):
                    times(pr[:, :, w + 1:2 * w + 1], pi[:, :, w + 1:2 * w + 1], pr[:, :, 1:w + 1], pi[:, :, 1:w + 1],
                          pr[:, :, w:w + 1].broadcast_to([P, G, w]), pi[:, :, w:w + 1].broadcast_to([P, G, w]),
                          view(prep, 0, G, w), view(prep, 256, G, w))
                for d, src in ((prr, pr), (pir, pi)):
                    own(e.tensor_copy(d, src[:, :, 0:L5][:, :, ::-1]))
                own(TSC(bV[0:64], bV[0:64], -1.0, None, ALU.mult))
                tb = view(prep, 0, G, P5)
                mul(Bb, bU, wide(fr, P5))
                mul(tb, bV, wide(fi, P5))
                own(TTT(Bb, Bb, tb, ALU.add))
                mul(BV, bV, wide(fr, P5))
                mul(tb, bU, wide(fi, P5))
                own(TTT(BV, BV, tb, ALU.subtract))
                for out, U, V, p_r, p_i, n, name in ((WT, Bb, BV, prr, pir, L5, "wt_ok"), (CA, cU, cV, pr, pi, L5 + 1, "ca_ok")):
                    for g in range(0, G, 8):
                        gg = slice(g, g + 8)
                        tv = view(AR, 0, 8, n, P5)

                        def over_j(t):
                            return t[:, gg, None, :].broadcast_to([P, 8, n, P5])

                        def over_q(t):
                            return t[:, gg, :][:, :, :, None].broadcast_to([P, 8, n, P5])

                        mul(out[:, gg], over_j(U), over_q(p_r))
                        mul(tv, over_j(V), over_q(p_i))
                        own(TTT(out[:, gg], out[:, gg], tv, ALU.add))
                    e.sem_inc(S(name), 1)
                a8r, a8i = one_col(pr, 8), one_col(pi, 8)
                t8 = view(prep, 0, NB, G)
                mul(s1, x0, a8r[:, None, :].broadcast_to([P, NB, G]))
                mul(t8, x0s, a8i[:, None, :].broadcast_to([P, NB, G]))
                own(TTT(s1[0:64], s1[0:64], t8[0:64], ALU.subtract))
                own(TTT(s1[64:128], s1[64:128], t8[64:128], ALU.add))
                def double():
                    times(t0, t1, cs, sn, cs, sn, t2, dr)
                    mul(t2, t0, t0)
                    mul(dr, t1, t1)
                    own(TTT(t2, t2, dr, ALU.add))
                    own(TSC(t2, t2, -0.5, 1.5, ALU.mult, ALU.add))
                    mul(cs, t0, t2)
                    mul(sn, t1, t2)

                for _ in range(3):
                    double()
                own(e.memset(tc[:, :, 0:1], 1.0))
                own(e.memset(sg[:, :, 0:1], 0.0))
                for w in (1, 2, 4, 8, 16, 32):
                    times(tc[:, :, w:2 * w], sg[:, :, w:2 * w], tc[:, :, 0:w], sg[:, :, 0:w], wide(cs, w), wide(sn, w),
                          view(AR, 0, G, w), view(AR, 2048, G, w))
                    if w < 32:
                        double()
                own(TSC(sg[64:128], sg[64:128], -1.0, None, ALU.mult))
                e.sem_inc(S("tables_ok"), 1)
            sums(0)
            s5_parameters()
            sums(1)
            e.wait_ge(mm_done, groups[W_IN]["n0"] + 2)
            e.memset(TT, 0.0).then_inc(S("tt_zero"), 1)
            e.wait_ge(mm_done, groups[W_OUT]["n0"] + 2)
            e.memset(wglu, 0.0).then_inc(S("tt_zero"), 1)
            mark(TTT(keep5, sm[:, 4, :][:, :, None].broadcast_to([P, G, C5P]),
                chunk_keep[:, None, :].broadcast_to([P, G, C5P]), ALU.mult), "keep_ok")
            e.wait_ge(ps_free, groups[W_OUT]["n0"] + 2)
            mark(TSC(PR[:, 0:2, :], PR[:, 0:2, :], DK ** -0.5, None, ALU.mult), "q_ok")
            e.wait_ge(S("scan_ok"), 1)
            mark(e.memset(XS[:, :, 0:1], 0.0), "xs_ends")
            mark(e.tensor_copy(XS[:, :, C5P:C5], x0.rearrange("p b g -> p g b")), "xs_ends")
            e.wait_ge(S("mix_ok"), 4)
            e.wait_ge(S("zt_mm"), L5)
            e.wait_ge(S("s1_mm"), 1)
            mark(e.memset(SCp, 0.0), "sc_zero")
            mark(e.memset(SCs, 0.0), "sc_zero")
            for lv, hs in enumerate(LEVELS):
                TL, b = T if hs <= 4 else TP, (lv + 1) % 2
                e.wait_ge(S("e_ok"), lv + 1)
                if lv >= 1:
                    e.wait_ge(S("lev_mm"), lv)
                    e.wait_ge(S("ktok_mm"), NT)
                mark(TTT(gk[b][:, :, 0:TL], PR[:, 2:4, 0:TL], ge[b][:, :, 0:TL], ALU.mult), "lev_k")
                if lv == 0:
                    e.wait_ge(S("vtok_mm"), NT)
                    mark(e.memset(vtok[TS:P, NT - 1, :], 0.0), "v_zero")
            mark(e.memset(SC, 0.0), "sc_zero")
            mark(e.memset(Sall[:, :, 0, :], 0.0), "sc_zero")
            sums(2)
            e.wait_ge(mm_done, groups[W_O]["n0"] + 2)
            mark(e.memset(qz, 0.0), "qz_own")
            e.wait_ge(ps_free, groups[W_O]["n0"] + 2)
            for c in range(4):
                e.tensor_copy(qz[:, :, c::4, BT * c:BT * c + BT],
                              qT[:, :, TP:T].rearrange("p f (b t) -> p f b t", b=NB)[:, :, c::4, :]).then_inc(S("qz_ok"), 1)
            e.wait_ge(S("pv_mm"), 8)
            e.wait_ge(kv_out, 64)
            e.memset(PTz, 0.0).then_inc(S("ptz_zero"), 1)
            sums(3)
            sums(4)

        @block.tensor
        def _(e):
            mark = Mark(e)

            def mm(out, lhsT, rhs, start=True, stop=True, **kw):
                return e.matmul(out, lhsT, rhs, start=start, stop=stop, **kw)

            def dense(n, par, K, xa, xb, width=TH, parts=2, ready=None):
                e.wait_ge(w_lo, n + 3)
                e.wait_ge(ps_free, n + 1)
                last = None
                for k in range(K):
                    if ready:
                        e.wait_ge(ready[0], ready[1] + k + 1)
                    for wi, (w, x) in enumerate(((wh, xa), (wh, xb), (wl, xa))):
                        for j in range(parts):
                            last = mm(bank(2 * par + j, width), w[:, par, k * P:(k + 1) * P],
                                      x[:, k, j * width:(j + 1) * width],
                                      start=(k == 0 and wi == 0), stop=(k == K - 1 and wi == 2))
                last.then_inc(mm_done, 1)

            def dense_group(gi, xa, xb, ready=None, after_first=None, **kw):
                g = groups[gi]
                first = 0
                if ready or after_first:
                    first = 1
                    dense(g["n0"], 0, g["K"], xa, xb, ready=ready, **kw)
                    if after_first:
                        after_first()
                    dense(g["n0"] + 1, 1, g["K"], xa, xb, **kw)
                with e.Fori(first, g["n"] // 2) as i:
                    for par in range(2):
                        dense(i * 2 + (g["n0"] + par), par, g["K"], xa, xb, **kw)

            def mean_squares(src, mean, b):
                mm(bank(b, 512), mean[:], src[:, 0:512])
                return mm(bank(b + 1, T - 512), mean[:], src[:, 512:T])

            def rms(m):
                e.wait_ge(acc_ready, 8 * (m + 1))
                mean_squares(acc, mean_d, 4).then_inc(ss, 1)

            e.wait_ge(s_load, 7 * 16)
            e.wait_ge(s_const, 5)
            e.wait_ge(s_x, 32)
            for k in range(KD):
                if k >= 2:
                    e.wait_ge(x_ev, k - 1)
                for j in range(NT):
                    w = min(P, T - j * P)
                    last = e.transpose(bank(4 + 2 * (k % 2), w, at=j * P), xin[0:w, j, k * P:(k + 1) * P],
                                       ident[0:w, 0:w])
                last.then_inc(S("x_tr"), 1)

            def s5_turn():
                e.wait_ge(S("d_s5"), 16 * 12)
                e.transpose(bank(4, G), nat2[0:G, 0, :], ident[0:G, 0:G])
                e.transpose(bank(4, G, at=G), nat2[0:G, 1, :], ident[0:G, 0:G]).then_inc(S("lam_mm"), 1)
                for j in range(4):
                    last = e.transpose(bank(5, P, at=j * P), nat[:, j, :], ident)
                last.then_inc(S("c_mm"), 1)
                e.wait_ge(S("x0n_in"), 64)
                for j in range(2):
                    e.transpose(bank(6, P, at=j * P), x0n[:, j, :], ident)
                    last = e.transpose(bank(6, P, at=256 + j * P), x0sn[:, j, :], ident)
                last.then_inc(S("x0_mm"), 1)

            def s5_matrices():
                e.wait_ge(S("wt_ok"), 1)
                for r in range(8):
                    if r >= 2:
                        e.wait_ge(S("win_ok"), r - 1)
                    for j in range(4):
                        last = e.transpose(bank(4 + r % 2, P, at=j * P), WT[:, 4 * r + j, :, :].rearrange("p s q -> p (s q)"), ident)
                    last.then_inc(S("win_mm"), 1)
                e.wait_ge(S("ca_ok"), 1)
                for r in range(8):
                    if r >= 2:
                        e.wait_ge(S("kt_ok"), r - 1)
                    for j in range(4):
                        g = 4 * r + j
                        last = mm(bank(6 + r % 2, P, at=j * P, rows=P5), Bb[:, g, :],
                                  CA[:, g, 0:L5, :].rearrange("p j q -> p (j q)"))
                    last.then_inc(S("kt_mm"), 1)
                e.wait_ge(S("win_ok"), 8)
                e.wait_ge(S("kt_ok"), 8)

            def ffn_pe(first, m):
                done = groups[first]["f0"]
                for i, nf in enumerate(FGROUPS):
                    if i == 0:
                        dense_group(first, xh, xl, ready=(x_lo, 8 * m), after_first=lambda: rms(m))
                    else:
                        dense_group(first + 2 * i, xh, xl)
                    if first == 0 and i == 0:
                        s5_turn()
                    dense_group(first + 2 * i + 1, yh, yl, ready=(hid_lo, done))
                    done += nf

            ffn_pe(0, 0)
            s5_matrices()
            dense_group(W_IN, xh, xl, ready=(x_lo, 8), after_first=lambda: rms(1))
            dense_group(W_IN + 1, xh, xl)
            e.wait_ge(S("wzg_ok"), 1)
            for k in range(KD):
                for j in range(2):
                    last = mm(bank(6 + j, TH, rows=RANK), wzg[:, k, :], h[:, k, j * TH:(j + 1) * TH],
                              start=k == 0, stop=k == KD - 1)
            last.then_inc(S("zg_mm"), 1)
            e.wait_ge(ps_free, groups[W_OUT]["n0"] + 2)
            for s in range(L5):
                if s >= 2:
                    e.wait_ge(S("ut_ok"), s - 1)
                for j in range(4):
                    last = e.transpose(bank(s % 2, P, at=j * P, rows=C5), PR[:, 12 + j, s::L5], ident)
                last.then_inc(S("ut_mm"), 1)
            e.wait_ge(S("ut_ok"), L5)
            for r in range(5):
                if r >= 2:
                    e.wait_ge(S("u2_ok"), r - 1)
                for j in range(7 * r, min(G, 7 * r + 7)):
                    last = e.transpose(bank(2 + r % 2, C5, at=(j % 7) * C5),
                                       UT[:, j, :, :].rearrange("p s q -> p (s q)"), ident[0:C5, 0:C5])
                last.then_inc(S("u2_mm"), 1)
            e.wait_ge(S("zg_ok"), 1)
            e.wait_ge(S("u2_ok"), 5)
            e.wait_ge(S("zg_ok"), 1)
            e.wait_ge(S("d_gla"), 16 * 3)
            for i in range(2):
                for j in range(2):
                    last = mm(bank(2 * i + j, TH), wgate[0:RANK, i * P:(i + 1) * P], zg[0:RANK, j * TH:(j + 1) * TH])
            last.then_inc(S("z_mm"), 1)
            for r in range(5):
                if r >= 2:
                    e.wait_ge(S("d_ok"), r - 1)
                for j in range(7 * r, min(G, 7 * r + 7)):
                    at = (j % 7) * C5
                    mm(bank(4 + 2 * (r % 2), C5, at=at), Win[:, j, :], u2[:, j, :])
                    mm(PS[0:64, 5 + 2 * (r % 2), at:at + C5], Win[:, j, 64:128], u2[:, j, :])
                    last = mm(PS[64:128, 5 + 2 * (r % 2), at:at + C5], Win[:, j, 0:64], u2[:, j, :])
                last.then_inc(S("d_mm"), 1)
            e.wait_ge(S("tt_in"), 16 * L5)
            e.wait_ge(S("z_sb"), 2)
            for r in range(8):
                if r == 4:
                    e.wait_ge(S("d_ok"), 5)
                for j in range(4):
                    g = 4 * r + j
                    mm(bank(r, P, at=j * P, rows=C5), u2[:, g, :], TT[:, g, :], start=j == 0, stop=False, skip_group_check=True)
            e.wait_ge(S("xs_ends"), 2)
            for r in range(8):
                e.wait_ge(S("xs_ok"), r // 4 + 1)
                for j in range(4):
                    g = 4 * r + j
                    last = mm(bank(r, P, at=j * P, rows=C5), XS[:, g, :], CA[:, g, 1:, :].rearrange("p j q -> p (j q)"),
                              start=False, stop=True, skip_group_check=True)
                last.then_inc(S("y_mm"), 1)
            e.wait_ge(S("s1_ok"), 1)
            e.wait_ge(S("y_g"), 6)
            e.transpose(bank(2, P), s1[:, 0:4, :].rearrange("p b g -> p (b g)"), ident)
            e.transpose(bank(2, P, at=P), s1[:, 4:8, :].rearrange("p b g -> p (b g)"), ident)
            e.transpose(bank(2, P, at=2 * P, rows=G), sm[:, 14, :], ident).then_inc(S("s1_mm"), 1)
            e.wait_ge(S("y_g"), 16)
            e.wait_ge(S("s1o_ok"), 1)
            for s in range(L5):
                if s >= 2:
                    e.wait_ge(S("zt_ok"), s - 1)
                for j in range(4):
                    last = e.transpose(bank(4 + s % 2, C5, at=j * C5), Y2[:, s, j * P:(j + 1) * P], ident[0:C5, 0:C5])
                last.then_inc(S("zt_mm"), 1)
            e.wait_ge(S("zt_ok"), L5)
            e.wait_ge(S("glu_in"), 16 * 9)
            for f in range(4):
                if f >= 2:
                    e.wait_ge(S("sig_ok"), f - 1)
                for j in range(2):
                    last = mm(bank(2 * (f % 2) + j, TH), wglu[:, f, :], zT[:, f, j * TH:(j + 1) * TH])
                last.then_inc(S("glu_mm"), 1)
            for j in range(NT):
                if j >= 2:
                    e.wait_ge(S("vtok_ok"), j - 1)
                w = min(P, T - j * P)
                for f in range(4):
                    last = e.transpose(bank(6 + j % 2, P, at=f * P, rows=w), PR[:, 4 + f, j * P:j * P + w], ident)
                last.then_inc(S("vtok_mm"), 1)
            for r in range(len(LEVELS) + 1):
                qq, kk = (gq[r % 2], gk[r % 2]) if r else (PR[:, 0:2, :], PR[:, 2:4, :])
                if r:
                    e.wait_ge(S("lev_q"), r)
                    e.wait_ge(S("lev_k"), r)
                else:
                    e.wait_ge(S("q_ok"), 1)
                    e.wait_ge(S("sig_ok"), 4)
                if r >= 2:
                    e.wait_ge(S("lev_ok"), r - 1)
                nch = NCH + 1 if r <= 3 else NCH
                for c in range(nch):
                    for hd in range(H):
                        a, f = (hd % 2) * DK, hd // 2
                        o0 = (c % 2) * CH
                        last = mm(PS[o0:o0 + CH, 4 * (r % 2) + hd, (c // 2) * CH:(c // 2 + 1) * CH],
                                  kk[a:a + DK, f, c * CH:(c + 1) * CH], qq[a:a + DK, f, c * CH:(c + 1) * CH])
                last.then_inc(S("lev_mm"), 1)
                if r == 0:
                    e.wait_ge(S("ke_ok"), 1)
                    e.wait_ge(S("vtok_ok"), NT)
                    for j in range(NT):
                        if j >= 2:
                            e.wait_ge(S("ktok_ok"), j - 1)
                        w = min(P, T - j * P)
                        for f in range(2):
                            last = e.transpose(bank(6 + j % 2, P, at=f * P, rows=w), gk[0][:, f, j * P:j * P + w], ident)
                        last.then_inc(S("ktok_mm"), 1)
                    e.wait_ge(S("ktok_ok"), NT)
            e.wait_ge(S("kem_ok"), 1)
            e.wait_ge(S("v_zero"), 1)
            e.wait_ge(S("lev_ok"), 6)
            for c in range(NCH):
                for hd in range(H):
                    a, f = (hd % 2) * DK, hd // 2
                    o0 = (c % 2) * CH
                    last = mm(PS[a:a + DK, 4 + 2 * f + c % 2, (c // 2) * DV:(c // 2 + 1) * DV],
                              ktok[o0:o0 + CH, c // 2, hd * DK:(hd + 1) * DK],
                              vtok[o0:o0 + CH, c // 2, hd * DV:(hd + 1) * DV])
            last.then_inc(S("kv_mm"), 1)
            e.wait_ge(S("lev_ok"), 7)
            for b in range(NB):
                for hd in range(H):
                    a, f = (hd % 2) * DK, hd // 2
                    last = mm(PS[a:a + DK, 2 * f + b // 4, (b % 4) * DV:(b % 4 + 1) * DV],
                              kem[:, b, hd * DK:(hd + 1) * DK], vtok[0:TS, 4, hd * DV:(hd + 1) * DV])
            last.then_inc(S("kvs_mm"), 1)
            e.wait_ge(S("qe_ok"), 1)
            e.wait_ge(S("st_ok"), 1)
            e.wait_ge(S("sts_ok"), 1)
            e.wait_ge(S("sc_ok"), 1)
            for f in range(2):
                for hh in range(2):
                    hd, a = 2 * f + hh, hh * DK
                    B = 4 * f + 2 * hh
                    for c in range(1, NCH):
                        mm(bank(B, CH, at=c * CH), Sall[a:a + DK, f, c, :], gq[1][a:a + DK, f, c * CH:(c + 1) * CH],
                           start=(c == 1), stop=False, skip_group_check=True)
                    for b in range(NB):
                        t0 = TP + b * BT
                        mm(bank(B, BT, at=t0), S0[a:a + DK, f, b, :], gq[1][a:a + DK, f, t0:t0 + BT],
                           start=(b == 0), stop=False, skip_group_check=True)
                    for j in range(NT):
                        w = min(P, T - j * P)
                        last = mm(bank(B, w, at=j * P), vtok[:, j, hd * DV:(hd + 1) * DV], SC[:, hd, j, 0:w],
                                  start=False, stop=True, skip_group_check=True)
                    last.then_inc(S("o_mm"), 1)
            for hd in range(H):
                e.wait_ge(S("osq_ok"), hd + 1)
                mean_squares(osq[hd], mean_dv, 2 * hd).then_inc(S("oss_mm"), 1)
            e.wait_ge(S("mix_ok"), 8)
            dense_group(W_OUT, yh, yl)
            e.wait_ge(S("mem_ok"), 2)
            e.wait_ge(mm_done, groups[KV]["n0"] + 2)
            for k in range(KD):
                if k >= 2:
                    e.wait_ge(S("memx_lo"), k - 1)
                for j in range(2):
                    last = e.transpose(bank(4 + k % 2, P, at=j * P), mnat[:, j, k * P:(k + 1) * P], ident)
                last.then_inc(S("memt_mm"), 1)
            dense_group(KV, yh, yl, ready=(S("memx_lo"), 0), width=M, parts=1)
            e.wait_ge(ps_free, groups[W_Q]["n0"] + 2)
            for r in range(8):
                if r >= 2:
                    e.wait_ge(S("nat_ok"), r - 1)
                for j in range(4):
                    last = e.transpose(bank(4 + r % 2, P, at=j * P), KVT[:, 4 * (r % 4) + j, (r // 4) * P:(r // 4 + 1) * P], ident)
                last.then_inc(S("nat_mm"), 1)
            e.wait_ge(S("nat_ok"), 8)
            dense_group(W_Q, xh, xl, ready=(x_lo, 16), after_first=lambda: rms(2))
            e.wait_ge(ps_free, groups[W_O]["n0"] + 2)
            for j in range(4):
                for hd in range(H):
                    for f in range(2):
                        last = mm(bank(4, M, at=hd * M), qT[:, 2 * hd + f, j * P:(j + 1) * P], KVT[:, 2 * hd + f, :],
                                  start=f == 0, stop=f == 1)
                last.then_inc(S("s_mm"), 1)
                e.wait_ge(S("p_ok"), j + 1)
                for hd in range(H):
                    for f in range(2):
                        last = e.transpose(bank(6, P, at=(2 * hd + f) * P), pp[:, hd, f * P:(f + 1) * P], ident)
                last.then_inc(S("pt_mm"), 1)
            e.wait_ge(S("pt_ok"), 4)
            for f in range(8):
                if f >= 2:
                    e.wait_ge(S("pv_lo"), f - 1)
                for j in range(2):
                    last = mm(bank(4 + f % 2, TP), KVN[:, j, D + f * P:D + (f + 1) * P], PT[:, f // 2, j, :],
                              start=j == 0, stop=j == 1)
                last.then_inc(S("pv_mm"), 1)
            def turn_keys(b, half):
                if b:
                    e.wait_ge(S(("kbt_a", "kbt_v")[half]), b)
                for f in range(4 * half, 4 * half + 4):
                    for j in range(2):
                        last = e.transpose(bank(0, P, at=f * M + j * P), KB[b % 4][:, j, f * P:(f + 1) * P], ident)
                last.then_inc(S("kbt_mm"), 1)

            def turn_probs(c):
                e.wait_ge(S("p_ok"), 5 + c)
                for j in range(2):
                    last = e.transpose(bank(4 + c, P, at=j * P), pp[:, c, j * P:(j + 1) * P], ident)
                last.then_inc(S("pt_mm"), 1)

            e.wait_ge(S("pv_lo"), 8)
            e.wait_ge(S("kb_in0"), 16)
            turn_keys(0, 0)
            turn_keys(0, 1)
            e.wait_ge(S("qz_ok"), 4)
            for b in range(NB):
                for half in range(2):
                    e.wait_ge(S(("kbt_a", "kbt_v")[half]), b + 1)
                    for hd in (2 * half, 2 * half + 1):
                        for f in range(2):
                            last = mm(PS[32 * hd:32 * hd + 32, 6 + b // 4, 0:M], qz[:, 2 * hd + f, b, :],
                                      KBT[:, 2 * hd + f, :], start=(b % 4 == 0 and f == 0), stop=(b % 4 == 3 and f == 1),
                                      skip_group_check=True)
                    last.then_inc(S("ssm_mm"), 1)
                    if b + 1 < NB:
                        if half == 0:
                            e.wait_ge(S(f"kb_in{(b + 1) % 4}"), 16 * ((b + 1) // 4 + 1))
                        turn_keys(b + 1, half)
                    elif half == 0:
                        turn_probs(0)
            for c in range(2):
                if c:
                    turn_probs(1)
                e.wait_ge(S("pt_ok"), 5 + c)
                for b in range(4 * c, 4 * c + 4):
                    e.wait_ge(S(f"kb_in{b % 4}"), 16 * (b // 4 + 3))
                    for hd in range(H):
                        for j in range(2):
                            last = mm(PS[32 * hd:32 * hd + 32, c, 0:CD], PTz[:, j, hd, b, :],
                                      KB[b % 4][:, j, hd * CD:(hd + 1) * CD], start=(b % 4 == 0 and j == 0),
                                      stop=(b % 4 == 3 and j == 1), skip_group_check=True)
                    last.then_inc(S("pvs_mm"), 1)
            for c in range(2):
                e.wait_ge(S("os_ok"), c + 1)
                for f in range(2):
                    last = e.transpose(bank(2 + c, P, at=f * P), os[:, c, f * P:(f + 1) * P], ident)
                last.then_inc(S("ost_mm"), 1)
            e.wait_ge(S("pvs_lo"), 2)
            dense_group(W_O, yh, yl)
            ffn_pe(FFN2, 3)
            rms(4)
            for j in range(NT):
                e.wait_ge(S("yy_ok"), 8)
                if j >= 2:
                    e.wait_ge(S("yo_ok"), j - 1)
                w = min(P, T - j * P)
                for k in range(KD):
                    last = e.transpose(bank(2 * (j % 2), P, at=k * P, rows=w), yy[:, k, j * P:j * P + w], ident)
                last.then_inc(S("y_tr"), 1)

        @block.scalar
        def _(e):
            mark = Mark(e)

            def conv(gi, i, par):
                n0, K = groups[gi]["n0"], groups[gi]["K"]
                e.wait_ge(raw_in[par], i * 16 + (n0 // 2 * 16 + 16))
                e.wait_ge(mm_done, i * 2 + (n0 + par + 1))
                e.activation(wh[:, par, 0:K * P], raw[:, par, 0:K * P], ACT.Copy).then_inc(w_hi, 1)

            def group(gi, body, norm=None):
                g = groups[gi]

                def step(i, last, hook=None):
                    conv(gi, i, 1)
                    if hook:
                        hook()
                    body(i, i * 2 + g["n0"], 0)
                    if not last:
                        conv(gi, i + 1, 0)
                    elif gi + 1 < len(groups):
                        conv(gi + 1, 0, 0)
                    body(i, i * 2 + (g["n0"] + 1), 1)

                if norm is not None:
                    step(0, False, lambda: rms(norm))
                with e.Fori(0 if norm is None else 1, g["n"] // 2 - 1) as i:
                    step(i, False)
                step(g["n"] // 2 - 1, True)

            def norm_in(m, i, par):
                e.wait_ge(acc_ready, i * 2 + (8 * m + par - 1))
                k = i * 2 + par
                if m < 4:
                    e.activation(chunk(xh, k), chunk(h, k), ACT.Copy,
                                 scale=gains[:, gain_of[m], bass.ds(k, 1)]).then_inc(x_hi, 1)
                e.activation(sq[:, par, :], chunk(h, k), ACT.Square).then_inc(sq_ready, 1)

            def rms(m):
                e.wait_ge(ss, m + 1)
                e.activation(R[:], bank(4, T), ACT.Sqrt, bias=eps[:]).then_inc(rt, 1)

            def ffn(gi, m):
                for i in range(len(FGROUPS)):
                    g, d = groups[gi + 2 * i], groups[gi + 2 * i + 1]

                    def hidden(i, n, par, g=g):
                        if par == 0:
                            e.wait_ge(g_scaled, i + (g["f0"] + 1))
                            e.activation(act[:], gs[:], ACT.Silu).then_inc(g_act, 1)
                        else:
                            e.wait_ge(hid, i + (g["f0"] + 1))
                            e.activation(chunk(yh, i), us[:], ACT.Copy).then_inc(hid_hi, 1)

                    def down(i, n, par, d=d):
                        if d["norm"] is not None:
                            e.wait_ge(ps_free, n + 3)
                            norm_in(d["norm"], i, par)

                    group(gi + 2 * i, hidden, norm=m if i == 0 else None)
                    group(gi + 2 * i + 1, down)

            def nothing(i, n, par):
                pass

            conv(0, 0, 0)
            e.wait_ge(s_load, 7 * 16)
            e.wait_ge(s_const, 5)
            for k in range(KD):
                e.wait_ge(x_ev, k + 1)
                e.activation(xh[:, k, :], h[:, k, :], ACT.Copy, scale=gains[:, G_FFN1, k:k + 1]).then_inc(x_hi, 1)
                if k >= 2:
                    e.wait_ge(acc_ready, k - 1)
                e.activation(sq[:, k % 2, :], h[:, k, :], ACT.Square).then_inc(sq_ready, 1)
            e.wait_ge(S("x_tr"), KD)
            with nc.allow_non_contiguous_dma(reason="16-column rows of w_in, small parameters"):
                e.dma_start(wzg, A["w_in"][0, :, D:D + RANK].rearrange("(k p) r -> p k r", p=P)).then_inc(S("wzg_in"), 16)
                e.dma_start(wgate[0:RANK, :], A["w_gla_gate"][0]).then_inc(S("d_gla"), 16)
                e.dma_start(bgate, A["b_gla_gate"][0].rearrange("(f p) -> p f", p=P)).then_inc(S("d_gla"), 16)
                e.dma_start(ggla, A["g_gla_out"][0].rearrange("(p a) -> p a", a=1)).then_inc(S("d_gla"), 16)
                for a in range(2):
                    e.dma_start(nat2[0:G, 0, a * 64:(a + 1) * 64], A["s5_lambda_re"][0]).then_inc(S("d_s5"), 16)
                    e.dma_start(nat2[0:G, 1, a * 64:(a + 1) * 64], A["s5_lambda_im"][0]).then_inc(S("d_s5"), 16)
                e.dma_start(sm[:, 0, :], A["s5_log_dt"].broadcast_to([P, G])).then_inc(S("d_s5"), 16)
                for a, nm in enumerate(("s5_b_re", "s5_b_im")):
                    src = A[nm][0].rearrange("g n p -> n g p")
                    e.dma_start(bU[64 * a:64 * a + 64], src).then_inc(S("d_s5"), 16)
                    e.dma_start(bV[64 * (1 - a):64 * (1 - a) + 64], src).then_inc(S("d_s5"), 16)
                    e.dma_start(nat[:, :, 64 * a:64 * a + 64],
                                A[("s5_c_re", "s5_c_im")[a]][0].rearrange("(j g) p n -> (g p) j n", j=4)).then_inc(S("d_s5"), 16)
                e.dma_start(dd, A["s5_d"][0].rearrange("g p -> p g")).then_inc(S("d_s5"), 16)
                for a, nm in enumerate(("state_s5_re", "state_s5_im")):
                    src = A[nm][0].rearrange("(j b) g n -> (b g) j n", j=2)
                    e.dma_start(x0n[:, :, 64 * a:64 * a + 64], src).then_inc(S("x0n_in"), 16)
                    e.dma_start(x0sn[:, :, 64 * (1 - a):64 * (1 - a) + 64], src).then_inc(S("x0n_in"), 16)
                e.dma_start(bglu, A["s5_b_glu"][0].rearrange("(j g) p -> (g p) j", j=4)).then_inc(S("glu_in"), 16)
            ffn(0, 0)
            for r in range(8):
                e.wait_ge(S("win_mm"), r + 1)
                e.activation(Win[:, 4 * r:4 * r + 4, :], bank(4 + r % 2, 4, P), ACT.Copy).then_inc(S("win_ok"), 1)
            group(W_IN, nothing, norm=1)
            e.wait_ge(S("tt_zero"), 1)
            e.wait_ge(S("ktd_ok"), 1)
            for s in range(L5):
                e.dma_start(TT[P5 * s:P5 * s + P5, :, P5 * s:P], Kt[:, :, 0:P - P5 * s]).then_inc(S("tt_in"), 16)
            group(W_IN + 1, nothing)
            with nc.allow_non_contiguous_dma(reason="16 columns a row"):
                e.wait_ge(S("tt_zero"), 2)
                for gi in range(8):
                    e.dma_start(wglu[16 * gi:16 * gi + 16, :, 16 * gi:16 * gi + 16],
                                A["s5_w_glu"][0].rearrange("(j g) p q -> g p j q", j=4)[gi]).then_inc(S("glu_in"), 16)
            for s in range(L5):
                e.wait_ge(S("ut_mm"), s + 1)
                e.activation(UT[:, :, s, :], bank(s % 2, G, P5, rows=C5), ACT.Copy).then_inc(S("ut_ok"), 1)
            e.wait_ge(S("z_sb"), 2)
            mark(e.activation(zt, zb, ACT.Abs), "act_own")
            mark(e.activation(zt, zt, ACT.Exp, scale=-1.0), "act_own")
            mark(e.activation(zt, zt, ACT.Ln, bias=one[:]), "ln_ok")
            for half in range(2):
                gg = slice(16 * half, 16 * half + 16)
                e.wait_ge(S("scan_ok"), 1)
                e.activation(zin[0:64, gg, :], zz[64:128, gg, :], ACT.Copy).then_inc(S("swap_a"), 1)
            e.wait_ge(S("s1_ok"), 1)
            e.wait_ge(S("swap_a"), 2)
            for r in range(8):
                e.wait_ge(S("y_mm"), r + 1)
                for t in range(2):
                    e.activation(Y2[:, 4 * t:4 * t + 4, 64 * r:64 * r + 64].rearrange("p t (g q) -> p g t q", g=4),
                                 bank(r, 4, L5, P5, rows=C5)[:, :, 4 * t:4 * t + 4, :], ACT.Gelu_apprx_tanh).then_inc(S("y_g"), 1)
            for f in range(4):
                e.wait_ge(S("glu_mm"), f + 1)
                if f:
                    e.wait_ge(S("so_ok"), f)
                e.activation(sig.rearrange("p (a t) -> p a t", a=2), PS[:, 2 * (f % 2):2 * (f % 2) + 2, 0:TH], ACT.Sigmoid,
                             bias=bglu[:, f:f + 1]).then_inc(S("sig_ok"), 1)
                e.wait_ge(S("so_ok"), f + 1)
                e.activation(yh[:, 4 + f, :], og, ACT.Copy).then_inc(S("mix_hi"), 1)
            e.wait_ge(S("s1o_ok"), 1)
            for a, nm in enumerate(("re", "im")):
                for j in range(2):
                    e.dma_start(O[f"s5_{nm}_s"][0].rearrange("(j b) g n -> j (b g) n", j=2)[j],
                                s1o[:, j, 64 * a:64 * a + 64]).then_inc(s5_out, 16)
                e.dma_start(O[f"s5_{nm}_p"][0, 0], s1o[0:G, 2, 64 * a:64 * a + 64]).then_inc(s5_out, 16)
            e.wait_ge(S("zt_mm"), L5)
            for f in range(2):
                e.dma_start(S0[:, f, :, :], A["state_gla"][0, :, 2 * f:2 * f + 2].rearrange("b q d e -> (q d) b e")).then_inc(S("s0_in"), 16)
            for j in range(NT):
                w = min(P, T - j * P)
                e.wait_ge(S("vtok_mm"), j + 1)
                e.activation(vtok[0:w, j, :], bank(6 + j % 2, 512, rows=w), ACT.Copy).then_inc(S("vtok_ok"), 1)
            e.wait_ge(S("ke_rel"), 2)
            e.activation(ge[0], ge[0], ACT.Exp, scale=1.0 / TAU).then_inc(S("ke_exp"), 1)
            for j in range(NT):
                w = min(P, T - j * P)
                e.wait_ge(S("ktok_mm"), j + 1)
                e.activation(ktok[0:w, j, :], bank(6 + j % 2, 2 * P, rows=w), ACT.Copy).then_inc(S("ktok_ok"), 1)
            for lv, hs in enumerate(LEVELS):
                TL = T if hs <= 4 else TP
                e.wait_ge(S("rel_ok"), lv + 1)
                d = ge[(lv + 1) % 2][:, :, 0:TL]
                mark(e.activation(d, d, ACT.Abs), "act_own")
                e.activation(d, d, ACT.Exp, scale=-1.0 / TAU).then_inc(S("e_ok"), 1)
            e.wait_ge(S("lev_q"), len(LEVELS) - 1)
            e.wait_ge(S("lev_k"), len(LEVELS) - 1)
            e.activation(ge[1], zb, ACT.Exp, scale=1.0 / TAU).then_inc(S("eb_ok"), 1)
            for hd in range(H):
                e.wait_ge(S("o_sb"), hd + 1)
                e.wait_ge(S("o_mm"), H)
                e.activation(osq[hd], oT[:, hd, :], ACT.Square).then_inc(S("osq_ok"), 1)
            for hd in range(2):
                e.wait_ge(S("oss_mm"), hd + 1)
                e.activation(oroot[hd], bank(2 * hd, T), ACT.Sqrt, bias=eps[:]).then_inc(S("ort"), 1)
            for hd in range(H):
                if hd:
                    e.wait_ge(S("og_ok"), hd)
                e.activation(act[:], PR[:, 8 + hd, :], ACT.Silu).then_inc(S("rs_ok"), 1)
                e.wait_ge(S("og_ok"), hd + 1)
                e.activation(yh[:, hd, :], us[:], ACT.Copy).then_inc(S("mix_hi"), 1)
                if hd < 2:
                    e.wait_ge(S("oss_mm"), hd + 3)
                    e.activation(oroot[hd], bank(2 * hd + 4, T), ACT.Sqrt, bias=eps[:]).then_inc(S("ort"), 1)
            e.wait_ge(S("st_ok"), 1)
            e.wait_ge(S("snew_ok"), 1)
            for f in range(2):
                e.dma_start(O["gla_p"][0, 0, 2 * f:2 * f + 2].rearrange("q d e -> (q d) e"), Sall[:, f, NCH, :]).then_inc(gla_out, 16)
                e.dma_start(O["gla_s"][0, :, 2 * f:2 * f + 2].rearrange("b q d e -> (q d) b e"), Snew[:, f, :, :]).then_inc(gla_out, 16)
            e.wait_ge(gla_out, 64)
            e.wait_ge(S("oss_mm"), H)
            e.dma_start(mnat, A["mem_prompt"][0].rearrange("(j p) d -> p j d", p=P)).then_inc(S("mem_in"), 16)

            def norm2(i, n, par):
                e.wait_ge(ps_free, n + 3)
                norm_in(2, i, par)

            group(W_OUT, norm2)
            e.wait_ge(S("mem_in"), 16)
            for j in range(2):
                mark(e.activation(msq, mnat[:, j, :], ACT.Square, accum_out=mst[:, j:j + 1]), "act_own")
            e.activation(mst[:, 2:4], mst[:, 0:2], ACT.Sqrt, bias=eps[:], scale=1.0 / D).then_inc(S("mrt"), 1)
            e.wait_ge(mm_done, groups[KV]["n0"] + 2)
            for k in range(KD):
                e.wait_ge(S("memt_mm"), k + 1)
                e.activation(mh[:, k, :], bank(4 + k % 2, M), ACT.Copy, scale=gains[:, G_MEM, k:k + 1]).then_inc(S("memx_hi"), 1)
            group(KV, nothing)
            e.wait_ge(S("nat_ok"), 8)
            for j in range(2):
                for a, nm in enumerate(("mem_k", "mem_v")):
                    e.dma_start(O[nm][0, 0, j * P:(j + 1) * P].rearrange("m h d -> m (h d)"),
                                KVN[:, j, a * D:(a + 1) * D]).then_inc(kv_out, 16)
            group(W_Q, nothing, norm=2)

            def softmax(r, w):
                e.wait_ge(S("mx_ok"), r + 1)
                if r:
                    e.wait_ge(S("pt_mm"), r)
                for hd in range(H):
                    e.activation(pp[0:w, hd, :], bank(4, H, M, rows=w)[:, hd, :], ACT.Exp, bias=att[0:w, 4 + hd:5 + hd],
                                 scale=CD ** -0.5, accum_out=att[0:w, 8 + hd:9 + hd]).then_inc(S("exp_ok"), 1)

            def softmax_decode(c):
                e.wait_ge(S("mx_ok"), 5 + c)
                e.activation(pp[:, c, :], bank(6 + c, M), ACT.Exp, bias=att[:, 4 + c:5 + c],
                             scale=CD ** -0.5, accum_out=att[:, 8 + c:9 + c]).then_inc(S("exp_ok"), 1)

            for r in range(4):
                softmax(r, P)
            for f in range(8):
                e.wait_ge(S("pv_mm"), f + 1)
                e.activation(yh[:, f, 0:TP], bank(4 + f % 2, TP), ACT.Copy).then_inc(S("pv_hi"), 1)
            e.wait_ge(kv_out, 64)
            for b in range(NB):
                e.wait_ge(S("kbt_mm"), 2 * b + 1)
                if b:
                    e.wait_ge(S("ssm_mm"), 2 * b - 1)
                e.activation(KBT[:, 0:4, :].rearrange("p f m -> p (f m)"), bank(0, 1024), ACT.Copy).then_inc(S("kbt_a"), 1)
                if b == 5:
                    softmax_decode(0)
            softmax_decode(1)
            for c in range(2):
                e.wait_ge(S("ost_mm"), c + 1)
                e.activation(yh[:, :, TP + 32 * c:TP + 32 * c + 32].rearrange("p (h f) t -> p f h t", f=2),
                             bank(2 + c, 2, H, 32), ACT.Copy).then_inc(S("pvs_hi"), 1)

            def norm3(i, n, par):
                e.wait_ge(ps_free, n + 3)
                norm_in(3, i, par)

            group(W_O, norm3)
            ffn(FFN2, 3)
            rms(4)
            for j in range(NT):
                w = min(P, T - j * P)
                e.wait_ge(S("yo_ok"), j + 1)
                dst = O["y_p"][0, j * P:(j + 1) * P, :] if j < 4 else O["y_s"].rearrange("b t d -> (b t) d")
                e.dma_start(dst, yo[0:w, j % 2, :]).then_inc(y_out[j % 2], 16)
            e.wait_ge(y_out[0], 16 * 3)
            e.wait_ge(y_out[1], 16 * 2)
            e.wait_ge(s5_out, 16 * 6)

        @block.vector
        def _(e):
            mark = Mark(e)
            TTT, TSC, STT, CP = e.tensor_tensor, e.tensor_scalar, e.scalar_tensor_tensor, e.tensor_copy

            def own(ins):
                mark(ins, "dve_own")

            def conv(gi, i, par):
                n0, K = groups[gi]["n0"], groups[gi]["K"]
                e.wait_ge(w_hi, i * 2 + (n0 + par + 1))
                TTT(wl[:, par, 0:K * P], raw[:, par, 0:K * P], wh[:, par, 0:K * P].bitcast(F32), ALU.subtract).then_inc(w_lo, 1)

            def group(gi, body, norm=None):
                g = groups[gi]

                def step(i, last, hook=None):
                    conv(gi, i, 1)
                    if hook:
                        hook()
                    e.wait_ge(mm_done, i * 2 + (g["n0"] + 3))
                    body(i, i * 2 + g["n0"], 0)
                    if not last:
                        conv(gi, i + 1, 0)
                    elif gi + 1 < len(groups):
                        conv(gi + 1, 0, 0)
                    e.wait_ge(mm_done, i * 2 + (g["n0"] + 4))
                    body(i, i * 2 + (g["n0"] + 1), 1)

                if norm is not None:
                    step(0, False, lambda: rms(norm))
                with e.Fori(0 if norm is None else 1, g["n"] // 2 - 1) as i:
                    step(i, False)
                step(g["n"] // 2 - 1, True)

            def halves(b):
                return PS[:, b:b + 2, 0:TH]

            def two(ap):
                return ap.rearrange("p (a t) -> p a t", a=2)

            def norm_in(m, i, par):
                k = i * 2 + par
                if m < 4:
                    e.wait_ge(x_hi, i * 2 + (8 * m + par + 1))
                    STT(chunk(xl, k), chunk(h, k), gains[:, gain_of[m], bass.ds(k, 1)], chunk(xh, k).bitcast(F32),
                        ALU.mult, ALU.subtract).then_inc(x_lo, 1)

            def inverse(root, square, tmp, name):
                own(e.reciprocal(root, root))
                own(STT(tmp, root, -0.5, root, ALU.mult, ALU.mult))
                own(STT(tmp, square, EPS, tmp, ALU.add, ALU.mult))
                mark(STT(root, tmp, 1.5, root, ALU.add, ALU.mult), name)

            def rms(m):
                e.wait_ge(rt, m + 1)
                inverse(R[:], bank(4, T), gs[:], "r_ready")

            def down(g):
                def body(i, n, par):
                    k = i * 2 + par
                    hk = chunk(h, k)
                    STT(two(hk), halves(2 * par), 0.5 if g["half"] else 1.0, two(hk), ALU.mult, ALU.add).then_inc(ps_free, 1)
                    if g["norm"] is not None:
                        e.wait_ge(ps_free, n + 3)
                        norm_in(g["norm"], i, par)
                return body

            def ffn(gi, m):
                for i in range(len(FGROUPS)):
                    g = groups[gi + 2 * i]

                    def hidden(i, n, par, g=g):
                        if par == 0:
                            TTT(two(gs[:]), halves(0), two(R[:]), ALU.mult).then_inc(g_scaled, 1)
                            e.wait_ge(g_scaled, i + (g["f0"] + 1))
                            e.sem_inc(ps_free, 1)
                        else:
                            TTT(two(us[:]), halves(2), two(R[:]), ALU.mult).then_inc(ps_free, 1)
                            e.wait_ge(ps_free, n + 3)
                            e.wait_ge(g_act, i + (g["f0"] + 1))
                            TTT(us[:], us[:], act[:], ALU.mult).then_inc(hid, 1)
                            e.wait_ge(hid, i + (g["f0"] + 1))
                            e.wait_ge(hid_hi, i + (g["f0"] + 1))
                            TTT(chunk(yl, i), us[:], chunk(yh, i).bitcast(F32), ALU.subtract).then_inc(hid_lo, 1)

                    group(gi + 2 * i, hidden, norm=m if i == 0 else None)
                    if gi == 0 and i == 0:
                        s5_turned()
                    group(gi + 2 * i + 1, down(groups[gi + 2 * i + 1]))

            def s5_turned():
                e.wait_ge(S("lam_mm"), 1)
                mark(CP(sm[:, 7:9, :], bank(4, 2, G)), "prep_in")
                own(TTT(sm[:, 12:14, :], sm[:, 7:9, :], sm[:, 7:9, :], ALU.mult))
                own(TTT(sm[:, 14, :], sm[:, 12, :], sm[:, 13, :], ALU.add))
                mark(e.reciprocal(sm[:, 14, :], sm[:, 14, :]), "prep_in")
                e.wait_ge(S("c_mm"), 1)
                cc = bank(5, G, P5)
                mark(CP(cU[0:64], cc[0:64]), "prep_in")
                mark(TSC(cU[64:128], cc[64:128], -1.0, None, ALU.mult), "prep_in")
                mark(TSC(cV[0:64], cc[64:128], -1.0, None, ALU.mult), "prep_in")
                mark(TSC(cV[64:128], cc[0:64], -1.0, None, ALU.mult), "prep_in")
                e.wait_ge(S("x0_mm"), 1)
                mark(CP(x0, bank(6, NB, G)), "prep_in")
                mark(CP(x0s, bank(6, NB, G, at=256)), "prep_in")

            e.sem_inc(w_lo, 2)
            e.sem_inc(mm_done, 2)
            e.sem_inc(ps_free, 2)
            conv(0, 0, 0)
            e.wait_ge(s_load, 7 * 16)
            for k in range(KD):
                e.wait_ge(S("x_tr"), k + 1)
                mark(CP(h[:, k, :], bank(4 + 2 * (k % 2), T)), "x_ev")
                e.wait_ge(x_hi, k + 1)
                STT(xl[:, k, :], h[:, k, :], gains[:, G_FFN1, k:k + 1], xh[:, k, :].bitcast(F32), ALU.mult, ALU.subtract).then_inc(x_lo, 1)
            ffn(0, 0)
            for r in range(8):
                e.wait_ge(S("kt_mm"), r + 1)
                mark(CP(Kt[:, 4 * r:4 * r + 4, :], bank(6 + r % 2, 4, P, rows=P5)), "kt_ok")
            own(TTT(ktmp, ident[0:P5, None, 0:P5].broadcast_to([P5, G, P5]), dd[:, :, None].broadcast_to([P5, G, P5]), ALU.mult))
            mark(TTT(Kt[:, :, 0:P5], Kt[:, :, 0:P5], ktmp, ALU.add), "ktd_ok")
            e.wait_ge(S("wzg_in"), 16)
            e.wait_ge(s_load, 7 * 16)
            mark(TTT(wzg, wzg, gains[:, G_MIX, :][:, :, None].broadcast_to([P, KD, RANK]), ALU.mult), "wzg_ok")

            def proj(f0, scales):
                def body(i, n, par):
                    f = i * 2 + (f0 + par)
                    TTT(two(chunk(PR, f)), halves(2 * par), two(R[:]), ALU.mult).then_inc(ps_free, 1)
                return body

            group(W_IN, proj(0, True), norm=1)
            e.wait_ge(S("tt_in"), 16 * L5)
            group(W_IN + 1, proj(8, False))
            e.wait_ge(S("zg_mm"), 1)
            mark(TTT(two(zg[0:RANK, :]), PS[0:RANK, 6:8, 0:TH], two(R[0:RANK, :]), ALU.mult), "zg_ok")
            e.wait_ge(S("tables_ok"), 1)

            def one_col(t, j):
                return t[:, :, j:j + 1].rearrange("p g a -> p (g a)")

            for r in range(5):
                n = min(G, 7 * r + 7) - 7 * r
                e.wait_ge(S("u2_mm"), r + 1)
                mark(CP(u2[:, 7 * r:7 * r + n, :], bank(2 + r % 2, n, C5)), "u2_ok")
            e.wait_ge(S("z_mm"), 1)
            for i in range(2):
                mark(TSC(two(zb[:, i, :]), halves(2 * i), bgate[:, i:i + 1], None, ALU.add), "z_sb")
            for r in range(5):
                n = min(G, 7 * r + 7) - 7 * r
                gg = slice(7 * r, 7 * r + n)
                if r == 2:
                    e.wait_ge(S("ln_ok"), 1)
                    own(STT(zt, zb, 0.0, zt, ALU.min, ALU.subtract))
                    for i in range(2):
                        own(e.tensor_tensor_scan(zb[:, i, :], scan_keep, zt[:, i, :], 0.0, ALU.mult, ALU.add))
                e.wait_ge(S("d_mm"), r + 1)
                d, dw = bank(4 + 2 * (r % 2), n, C5), bank(5 + 2 * (r % 2), n, C5)
                tw = view(zin_tmp, 0, n, C5P)
                own(TTT(zin[:, gg, :], d[:, :, 0:C5P], tc[:, gg, :], ALU.mult))
                own(TTT(tw, dw[:, :, 0:C5P], sg[:, gg, :], ALU.mult))
                own(TTT(zin[:, gg, :], zin[:, gg, :], tw, ALU.add))
                mark(TTT(s1[:, :, gg].rearrange("p b g -> p g b"), d[:, :, C5P:C5], s1[:, :, gg].rearrange("p b g -> p g b"), ALU.add), "d_ok")
            fl = "p g c -> p (g c)"
            e.wait_ge(S("keep_ok"), 1)
            mark(e.tensor_tensor_scan(zz.rearrange(fl), keep5.rearrange(fl), zin.rearrange(fl), 0.0, ALU.mult, ALU.add), "scan_ok")
            for half in range(2):
                gg = slice(16 * half, 16 * half + 16)
                own(CP(zin[64:128, gg], zz[0:64, gg]))
                e.wait_ge(S("swap_a"), half + 1)
                own(TTT(zin[:, gg], zin[:, gg], sg[:, gg], ALU.mult))
                own(TTT(zz[:, gg], zz[:, gg], tc[:, gg], ALU.mult))
                mark(TTT(XS[:, gg, 1:C5P], zz[:, gg, 0:C5P - 1], zin[:, gg, 0:C5P - 1], ALU.subtract), "xs_ok")
            own(TTT(sm[:, 14, :], one_col(zz, C5P - 1), one_col(zin, C5P - 1), ALU.subtract))
            e.sem_inc(S("s1_ok"), 1)
            e.wait_ge(S("s1_mm"), 1)
            own(CP(s1o[:, 0:2, :], bank(2, 2, P)))
            mark(CP(s1o[0:G, 2, :], bank(2, P, at=2 * P, rows=G)), "s1o_ok")
            for j in range(L5):
                e.wait_ge(S("zt_mm"), j + 1)
                mark(CP(zT[:, :, j::L5], bank(4 + j % 2, 4, C5)), "zt_ok")
            for f in range(4):
                e.wait_ge(S("sig_ok"), f + 1)
                mark(TTT(og, zT[:, f, :], sig, ALU.mult), "so_ok")
                e.wait_ge(S("mix_hi"), 1 + f)
                mark(TTT(yl[:, 4 + f, :], og, yh[:, 4 + f, :].bitcast(F32), ALU.subtract), "mix_ok")
            q, k_ = PR[:, 0:2, :], PR[:, 2:4, :]
            def against(dst, t0, t1, size, at):
                n = (t1 - t0) // size
                bb = zb[:, :, t0:t1].rearrange("p a (n s) -> p a n s", s=size)
                return TTT(dst[:, :, t0:t1].rearrange("p a (n s) -> p a n s", s=size),
                           bb[:, :, :, at:at + 1].broadcast_to([P, 2, n, size]), bb, ALU.subtract)

            mark(against(ge[0], 0, TP, CH, CH - 1), "ke_rel")
            mark(against(ge[0], TP, T, BT, BT - 1), "ke_rel")

            def level_rel(lv):
                hs = LEVELS[lv]
                if lv >= 2:
                    e.wait_ge(S("lev_k"), lv - 1)
                mark(against(ge[(lv + 1) % 2], 0, T if hs <= 4 else TP, 2 * hs, hs - 1), "rel_ok")

            level_rel(0)
            e.wait_ge(S("ke_exp"), 1)
            mark(TTT(gk[0], k_, ge[0], ALU.mult), "ke_ok")
            e.wait_ge(S("sc_zero"), 2)

            def take(r):
                b = 4 * (r % 2)
                e.wait_ge(S("lev_mm"), r + 1)
                own(e.copy_predicated(SCp, level_mask[:, r, :][:, None, None, :].broadcast_to([P, H, 4, CH]),
                                      PS[:, b:b + 4, 0:256].rearrange("p h (j t) -> p h j t", j=4)))
                if r <= 3:
                    own(e.copy_predicated(SCs[0:TS], level_mask[0:TS, r, :][:, None, :].broadcast_to([TS, H, CH]),
                                          PS[0:TS, b:b + 4, 256:320]))
                e.sem_inc(S("lev_ok"), 1)

            e.wait_ge(S("q_ok"), 1)
            for lv, hs in enumerate(LEVELS):
                TL, b = T if hs <= 4 else TP, (lv + 1) % 2
                if lv + 1 < len(LEVELS):
                    level_rel(lv + 1)
                e.wait_ge(S("e_ok"), lv + 1)
                if lv >= 2:
                    e.wait_ge(S("lev_mm"), lv)
                mark(TTT(gq[b][:, :, 0:TL], q[:, :, 0:TL], ge[b][:, :, 0:TL], ALU.mult), "lev_q")
                take(lv)
            take(len(LEVELS))
            e.wait_ge(S("sc_zero"), 4)
            for a in range(2):
                own(CP(SC[a * CH:(a + 1) * CH, :, 0:4, a * CH:(a + 1) * CH], SCp[a * CH:(a + 1) * CH]))
            mark(CP(SC[0:TS, :, 4, 0:CH], SCs[0:TS]), "sc_ok")
            e.wait_ge(S("eb_ok"), 1)
            mark(TTT(gq[1], q, ge[1], ALU.mult), "qe_ok")
            e.wait_ge(S("ktok_ok"), NT)
            e.wait_ge(S("vtok_ok"), NT)
            for b in range(NB):
                own(TSC(kem[:, b, :], ktok[0:TS, 4, :], batch_rows[0:TS, b:b + 1], None, ALU.mult))
            e.sem_inc(S("kem_ok"), 1)
            e.wait_ge(S("kv_mm"), 1)
            for c in range(NCH):
                for f in range(2):
                    own(STT(Sall[:, f, c + 1, :], Sall[:, f, c, :], ge[1][:, f, c * CH + CH - 1:c * CH + CH],
                            PS[:, 4 + 2 * f + c % 2, (c // 2) * DV:(c // 2 + 1) * DV], ALU.mult, ALU.add))
            e.sem_inc(S("st_ok"), 1)
            e.wait_ge(S("s0_in"), 32)
            e.wait_ge(S("kvs_mm"), 1)
            for b in range(NB):
                for f in range(2):
                    t1 = TP + b * BT + BT - 1
                    if b == 0 and f == 0:
                        e.wait_ge(s5_out, 16 * 6)
                    own(STT(Snew[:, f, b, :], S0[:, f, b, :], ge[1][:, f, t1:t1 + 1],
                            PS[:, 2 * f + b // 4, (b % 4) * DV:(b % 4 + 1) * DV], ALU.mult, ALU.add))
            e.sem_inc(S("sts_ok"), 1)
            e.sem_inc(S("snew_ok"), 1)
            for hd in range(H):
                e.wait_ge(S("o_mm"), hd + 1)
                mark(CP(oT[:, hd, :], bank(4 * (hd // 2) + 2 * (hd % 2), T)), "o_sb")
            for hd in range(H):
                e.wait_ge(S("oss_mm"), hd + 1)
                e.wait_ge(S("ort"), hd + 1)
                inverse(oroot[hd % 2], bank(2 * hd, T), gs[:], "orr_ok")
                if hd:
                    e.wait_ge(S("mix_hi"), 4 + hd)
                mark(STT(us[:], oT[:, hd, :], ggla[:, 0:1], oroot[hd % 2], ALU.mult, ALU.mult), "ous_ok")
                e.wait_ge(S("rs_ok"), hd + 1)
                mark(TTT(us[:], us[:], act[:], ALU.mult), "og_ok")
                e.wait_ge(S("mix_hi"), 4 + hd + 1)
                mark(TTT(yl[:, hd, :], us[:], yh[:, hd, :].bitcast(F32), ALU.subtract), "mix_ok")
            group(W_OUT, down(groups[W_OUT]))
            e.wait_ge(S("mrt"), 1)
            own(TSC(mst[:, 0:2], mst[:, 0:2], 1.0 / D, None, ALU.mult))
            inverse(mst[:, 2:4], mst[:, 0:2], mst[:, 4:6], "mst_ok")
            for j in range(2):
                mark(TSC(mnat[:, j, :], mnat[:, j, :], mst[:, 2 + j:3 + j], None, ALU.mult), "mem_ok")
            for k in range(KD):
                e.wait_ge(S("memx_hi"), k + 1)
                STT(ml[:, k, :], bank(4 + k % 2, M), gains[:, G_MEM, k:k + 1], mh[:, k, :].bitcast(F32),
                    ALU.mult, ALU.subtract).then_inc(S("memx_lo"), 1)

            def kv(i, n, par):
                CP(chunk(KVT, i * 2 + par), bank(2 * par, M)).then_inc(ps_free, 1)

            group(KV, kv)
            for r in range(8):
                e.wait_ge(S("nat_mm"), r + 1)
                mark(CP(KVN[:, r // 4, (r % 4) * 512:(r % 4 + 1) * 512], bank(4 + r % 2, 512)), "nat_ok")
            group(W_Q, proj(0, False), norm=2)

            def softmax(r, w):
                e.wait_ge(S("s_mm"), r + 1)
                own(e.tensor_reduce(att[0:w, 0:4], bank(4, H, M, rows=w), AX, ALU.max))
                mark(TSC(att[0:w, 4:8], att[0:w, 0:4], -(CD ** -0.5), None, ALU.mult), "mx_ok")
                e.wait_ge(S("exp_ok"), H * (r + 1))
                own(e.reciprocal(att[0:w, 12:16], att[0:w, 8:12]))
                for hd in range(H):
                    own(TSC(pp[0:w, hd, :], pp[0:w, hd, :], att[0:w, 12 + hd:13 + hd], None, ALU.mult))
                e.sem_inc(S("p_ok"), 1)
                e.wait_ge(S("pt_mm"), r + 1)

            for r in range(4):
                softmax(r, P)
                mark(CP(PT[:, :, :, r * P:(r + 1) * P].rearrange("p h j t -> p (h j) t"), bank(6, 8, P)), "pt_ok")
            for f in range(8):
                e.wait_ge(S("pv_hi"), f + 1)
                mark(TTT(yl[:, f, 0:TP], bank(4 + f % 2, TP), yh[:, f, 0:TP].bitcast(F32), ALU.subtract), "pv_lo")

            def decode_max(c):
                e.wait_ge(S("ssm_mm"), 8 * (c + 1))
                own(e.tensor_reduce(att[:, c:c + 1], bank(6 + c, M), AX, ALU.max))
                mark(TSC(att[:, 4 + c:5 + c], att[:, c:c + 1], -(CD ** -0.5), None, ALU.mult), "mx_ok")

            def decode_probs(c):
                e.wait_ge(S("exp_ok"), 4 * H + c + 1)
                own(e.reciprocal(att[:, 12 + c:13 + c], att[:, 8 + c:9 + c]))
                mark(TSC(pp[:, c, :], pp[:, c, :], att[:, 12 + c:13 + c], None, ALU.mult), "p_ok")

            def decode_turned(c):
                e.wait_ge(S("pt_mm"), 5 + c)
                e.wait_ge(S("ptz_zero"), 1)
                for q in range(4):
                    own(CP(PTz[:, :, :, 4 * c + q, BT * q:BT * q + BT], bank(4 + c, 2, H, 4, BT)[:, :, :, q, :]))
                e.sem_inc(S("pt_ok"), 1)

            for b in range(NB):
                e.wait_ge(S("kbt_mm"), 2 * b + 2)
                if b:
                    e.wait_ge(S("ssm_mm"), 2 * b)
                mark(CP(KBT[:, 4:8, :].rearrange("p f m -> p (f m)"), bank(2, 1024)), "kbt_v")
                if b == 4:
                    decode_max(0)
                if b == 6:
                    decode_probs(0)
            decode_turned(0)
            decode_max(1)
            decode_probs(1)
            decode_turned(1)
            for c in range(2):
                e.wait_ge(S("pvs_mm"), 4 * (c + 1))
                mark(CP(os[:, c, :], bank(c, M)), "os_ok")
            for c in range(2):
                e.wait_ge(S("pvs_hi"), c + 1)
                tt = slice(TP + 32 * c, TP + 32 * c + 32)
                mark(TTT(yl[:, :, tt].rearrange("p (h f) t -> p f h t", f=2), bank(2 + c, 2, H, 32),
                         yh[:, :, tt].bitcast(F32).rearrange("p (h f) t -> p f h t", f=2), ALU.subtract), "pvs_lo")
            group(W_O, down(groups[W_O]))
            ffn(FFN2, 3)
            rms(4)
            for k in range(KD):
                mark(STT(yy[:, k, :], h[:, k, :], gains[:, G_FINAL, k:k + 1], R[:], ALU.mult, ALU.mult), "yy_ok")
            for j in range(NT):
                w = min(P, T - j * P)
                e.wait_ge(S("y_tr"), j + 1)
                if j >= 2:
                    e.wait_ge(y_out[j % 2], 16 * (j // 2))
                mark(CP(yo[0:w, j % 2, :], bank(2 * (j % 2), D, rows=w)), "yo_ok")


_INS = ["x_prompt", "x_sample", "state_gla", "state_s5_re", "state_s5_im", "cache_mem_k", "cache_mem_v", "mem_prompt",
        "g_ffn1", "w_ffn1_gu", "w_ffn1_down", "g_mix", "w_in", "w_gla_gate", "b_gla_gate", "g_gla_out", "s5_lambda_re",
        "s5_lambda_im", "s5_log_dt", "s5_b_re", "s5_b_im", "s5_c_re", "s5_c_im", "s5_d", "s5_w_glu", "s5_b_glu", "w_out",
        "g_cross", "g_mem", "w_cq", "w_ckv", "w_co", "g_ffn2", "w_ffn2_gu", "w_ffn2_down", "g_final"]
_OUTS = [("y_p", (1, TP, D)), ("y_s", (NB, BT, D)), ("gla_p", (1, 1, H, DK, DV)), ("s5_re_p", (1, 1, G, N5)),
         ("s5_im_p", (1, 1, G, N5)), ("mem_k", (1, 1, M, H, CD)), ("mem_v", (1, 1, M, H, CD)),
         ("gla_s", (1, NB, H, DK, DV)), ("s5_re_s", (1, NB, G, N5)), ("s5_im_s", (1, NB, G, N5))]


def constants():
    import numpy as np
    c = np.zeros((P, C_END), np.float32)
    c[:, C_ID:C_ID + P] = np.eye(P)
    t = np.arange(T)
    c[:, C_SCAN:C_SCAN + T] = np.where(t < TP, t % CH, t % BT) != 0
    s, u = np.arange(P)[:, None] % CH, np.arange(CH)[None, :]
    levels = [s == u] + [(s // (2 * n) == u // (2 * n)) & (s % (2 * n) < n) & (u % (2 * n) >= n) for n in LEVELS]
    c[:, C_MASK:C_MASK + 7 * CH] = np.concatenate(levels, axis=1)
    c[:, C_CHUNK:C_CHUNK + C5P] = np.arange(C5P) != 0
    c[:, C_BATCH:C_BATCH + NB] = np.arange(P)[:, None] // BT == np.arange(NB)[None, :]
    return c


def kernel(**inputs):
    import numpy as _np
    import concourse.bacc as _bacc
    from concourse import mybir as _mybir
    from concourse.bass_utils import run_bass_kernel_spmd as _run

    nc = _bacc.Bacc("TRN2", target_bir_lowering=False, num_devices=1, dynamic_dma_scratch_size=1024)
    arrays, A, O = {}, {}, {}
    for name in _INS:
        a = _np.ascontiguousarray(inputs[name])
        arrays[f"in_{name}"] = a
        A[name] = nc.dram_tensor(f"in_{name}", a.shape, _mybir.dt.from_np(a.dtype), kind="ExternalInput").ap()
    c = constants()
    arrays["in_constants"] = c
    consts = nc.dram_tensor("in_constants", c.shape, _mybir.dt.float32, kind="ExternalInput").ap()
    for name, shape in _OUTS:
        O[name] = nc.dram_tensor(f"out_{name}", shape, _mybir.dt.float32, kind="ExternalOutput").ap()
    hymba_kernel(nc, A, O, consts)
    r = _run(nc, [arrays], core_ids=[0])
    return tuple(r.results[0][f"out_{name}"] for name, _ in _OUTS)
```
